# Optimizing a Trainium2 kernel written in Bass

```python
import jax, jax.numpy as jnp
from jax import lax
import numpy as np

D_MODEL = 1024
BATCH = 1
SEQ = 256
DEPTH = 2

N_A_LAYERS = DEPTH // 2
N_B_LAYERS = DEPTH - N_A_LAYERS
N_DENSE = (DEPTH + 1) // 2
N_MOE = DEPTH // 2
CONV_WIDTH = 3
ATT_GROUPS = ((128, 1), (512, 4), (2048, 16))
N_GROUPS = len(ATT_GROUPS)
HEAD_DIM = 64
HEADS_PER_GROUP = D_MODEL // 128
ATT_WIDTH = HEADS_PER_GROUP * HEAD_DIM
BLK = 128
D_FF = 11 * D_MODEL // 4
N_EXPERTS = 8
TOP_K = 2
D_EXPERT = 7 * D_MODEL // 2
ALPHA = (2.0 * DEPTH) ** 0.25
BETA = (8.0 * DEPTH) ** -0.25
LN_EPS = 1e-5

kernel_name = "hybrid_shortconv_dilatedattn_moe_deepnorm"

def layer_norm(x, g, b):
    xf = x.astype(jnp.float32)
    mu = jnp.mean(xf, axis=-1, keepdims=True)
    var = jnp.mean(jnp.square(xf - mu), axis=-1, keepdims=True)
    y = (xf - mu) * lax.rsqrt(var + LN_EPS) * g.astype(jnp.float32) + b.astype(jnp.float32)
    return y.astype(x.dtype)

def short_conv_mixer(x, w_in, conv_w, w_out):
    S = x.shape[1]
    gate_b, gate_c, u = jnp.split(jnp.einsum('bsd,dc->bsc', x, w_in), 3, axis=-1)
    u = gate_c * u
    up = jnp.pad(u, ((0, 0), (CONV_WIDTH - 1, 0), (0, 0)))
    conv = sum(conv_w[k] * up[:, k:k + S] for k in range(CONV_WIDTH))
    return jnp.einsum('bsc,cd->bsd', gate_b * conv, w_out)

def swiglu(x, w_gate, w_up, w_down):
    h = jax.nn.silu(jnp.einsum('bsd,df->bsf', x, w_gate)) * jnp.einsum('bsd,df->bsf', x, w_up)
    return jnp.einsum('bsf,fd->bsd', h, w_down)

def moe_swiglu(x, w_router, w_gate, w_up, w_down):
    logits = jnp.einsum('bsd,de->bse', x, w_router, preferred_element_type=jnp.float32)
    top_val, top_idx = lax.top_k(logits, TOP_K)
    gates = jax.nn.softmax(top_val, axis=-1)
    combine = jnp.einsum('bsk,bske->bse', gates,
                         jax.nn.one_hot(top_idx, N_EXPERTS, dtype=jnp.float32)).astype(x.dtype)
    out = jnp.zeros_like(x)
    for e in range(N_EXPERTS):
        out = out + combine[..., e:e + 1] * swiglu(x, w_gate[e], w_up[e], w_down[e])
    return out

def residue_blocks(t, d):
    B, S, H, E = t.shape
    L = -(-S // d)
    nblk = -(-L // BLK)
    Lp = nblk * BLK
    t = jnp.pad(t, ((0, 0), (0, d * Lp - S), (0, 0), (0, 0)))
    t = t.reshape(B, Lp, d, H, E).transpose(0, 2, 1, 3, 4)
    return t.reshape(B, d, nblk, BLK, H, E)

def from_residue_blocks(t, S):
    B, d, nblk, blk = t.shape[:4]
    rest = t.shape[4:]
    t = jnp.moveaxis(t.reshape((B, d, nblk * blk) + rest), 1, 2)
    return t.reshape((B, nblk * blk * d) + rest)[:, :S]

def banded(t):
    prev = jnp.pad(t, ((0, 0), (0, 0), (1, 0), (0, 0), (0, 0), (0, 0)))[:, :, :-1]
    return jnp.concatenate([prev, t], axis=3)

def band_mask(nblk, span):
    q = jnp.arange(BLK)[:, None]
    k = jnp.arange(2 * BLK)[None, :]
    dist = BLK + q - k
    n = jnp.arange(nblk)[:, None, None]
    return (dist >= 0) & (dist <= span) & ((n > 0) | (k >= BLK))

def shared_kv(x, kv_w):
    B, S, _ = x.shape
    kv = jnp.einsum('bsd,dc->bsc', x, kv_w).reshape(B, S, N_GROUPS, 2, HEADS_PER_GROUP, HEAD_DIM)
    blocks = []
    for g, (window, d) in enumerate(ATT_GROUPS):
        blocks.append((residue_blocks(kv[:, :, g, 0], d), residue_blocks(kv[:, :, g, 1], d)))
    return tuple(blocks)

def dilated_group_attention(q, k_res, v_res, d, span):
    S = q.shape[1]
    qb = residue_blocks(q, d)
    kb = banded(k_res)
    vb = banded(v_res)
    nblk = qb.shape[2]
    s = jnp.einsum('bdnqhe,bdnkhe->bdnhqk', qb, kb,
                   preferred_element_type=jnp.float32) * (HEAD_DIM ** -0.5)
    s = jnp.where(band_mask(nblk, span)[None, None, :, None], s, -jnp.inf)
    lse = jax.nn.logsumexp(s, axis=-1)
    p = jnp.exp(s - lse[..., None])
    o = jnp.einsum('bdnhqk,bdnkhe->bdnqhe', p.astype(vb.dtype), vb,
                   preferred_element_type=jnp.float32)
    o = from_residue_blocks(o, S)
    lse = from_residue_blocks(jnp.moveaxis(lse, 3, 4), S)
    return o, lse

def dilated_mixer(x, w_q, w_o, kv_blocks):
    B, S, _ = x.shape
    q = jnp.einsum('bsd,dc->bsc', x, w_q).reshape(B, S, N_GROUPS, HEADS_PER_GROUP, HEAD_DIM)
    outs, lses = [], []
    for g, (window, d) in enumerate(ATT_GROUPS):
        k_res, v_res = kv_blocks[g]
        o, lse = dilated_group_attention(q[:, :, g], k_res, v_res, d, window // d)
        outs.append(o)
        lses.append(lse)
    w = jax.nn.softmax(jnp.stack(lses, axis=-1), axis=-1)
    o = jnp.einsum('bshg,bshge->bshe', w, jnp.stack(outs, axis=3))
    o = o.reshape(B, S, ATT_WIDTH).astype(x.dtype)
    return jnp.einsum('bsc,cd->bsd', o, w_o)

def setup_inputs(seed: int = 0) -> dict:
    key = jax.random.key(seed)
    ks = jax.random.split(key, 16)
    D = D_MODEL

    def nrm(k, shape, fan_in, scale=1.0):
        return jax.random.normal(k, shape, jnp.float32) * (scale * fan_in ** -0.5)

    return {
        'x': jax.random.normal(ks[0], (BATCH, SEQ, D), jnp.float32),
        'a_w_in': nrm(ks[1], (N_A_LAYERS, D, 3 * D), D),
        'a_conv': nrm(ks[2], (N_A_LAYERS, CONV_WIDTH, D), CONV_WIDTH),
        'a_w_out': nrm(ks[3], (N_A_LAYERS, D, D), D, BETA),
        'kv_w': nrm(ks[4], (D, N_GROUPS * 2 * ATT_WIDTH), D),
        'b_w_q': nrm(ks[5], (N_B_LAYERS, D, N_GROUPS * ATT_WIDTH), D),
        'b_w_o': nrm(ks[6], (N_B_LAYERS, ATT_WIDTH, D), ATT_WIDTH, BETA),
        'ffn_w_gate': nrm(ks[7], (N_DENSE, D, D_FF), D),
        'ffn_w_up': nrm(ks[8], (N_DENSE, D, D_FF), D),
        'ffn_w_down': nrm(ks[9], (N_DENSE, D_FF, D), D_FF, BETA),
        'moe_w_router': nrm(ks[10], (N_MOE, D, N_EXPERTS), D),
        'moe_w_gate': nrm(ks[11], (N_MOE, N_EXPERTS, D, D_EXPERT), D),
        'moe_w_up': nrm(ks[12], (N_MOE, N_EXPERTS, D, D_EXPERT), D),
        'moe_w_down': nrm(ks[13], (N_MOE, N_EXPERTS, D_EXPERT, D), D_EXPERT, BETA),
        'ln_g': 1.0 + 0.02 * jax.random.normal(ks[14], (DEPTH, 2, D), jnp.float32),
        'ln_b': 0.02 * jax.random.normal(ks[15], (DEPTH, 2, D), jnp.float32),
    }

def reference(x, a_w_in, a_conv, a_w_out, kv_w, b_w_q, b_w_o, ffn_w_gate, ffn_w_up, ffn_w_down,
              moe_w_router, moe_w_gate, moe_w_up, moe_w_down, ln_g, ln_b):
    kv_blocks = None
    for l in range(DEPTH):
        if l < N_A_LAYERS:
            mix = short_conv_mixer(x, a_w_in[l], a_conv[l], a_w_out[l])
        else:
            if kv_blocks is None:
                kv_blocks = shared_kv(x, kv_w)
            j = l - N_A_LAYERS
            mix = dilated_mixer(x, b_w_q[j], b_w_o[j], kv_blocks)
        x = layer_norm(ALPHA * x + mix, ln_g[l, 0], ln_b[l, 0])
        i = l // 2
        if l % 2 == 0:
            ff = swiglu(x, ffn_w_gate[i], ffn_w_up[i], ffn_w_down[i])
        else:
            ff = moe_swiglu(x, moe_w_router[i], moe_w_gate[i], moe_w_up[i], moe_w_down[i])
        x = layer_norm(ALPHA * x + ff, ln_g[l, 1], ln_b[l, 1])
    return x


_drawn_inputs = setup_inputs


def setup_inputs(seed=0):
    import zlib

    import numpy as np

    out = dict(_drawn_inputs(seed))
    spreads = {}
    factors = {}
    for name, (base, spread) in spreads.items():
        noise = np.random.default_rng([zlib.crc32(name.encode()), seed]).standard_normal(out[name].shape)
        drawn = base * np.exp(spread * noise) if base else spread * noise
        out[name] = __import__('jax').numpy.asarray(drawn.astype(out[name].dtype))
    for name, factor in factors.items():
        out[name] = (out[name] * factor).astype(out[name].dtype)
    return out
```

```python
from contextlib import ExitStack

import concourse.bass as bass
from concourse import mybir

F32 = mybir.dt.float32
I32 = mybir.dt.int32
BF16 = mybir.dt.bfloat16
ALU = mybir.AluOpType
ACT = mybir.ActivationFunctionType
AX_X = mybir.AxisListType.X

P = 128
BANK = 512
ITEM = 2048
RING = 14
FAR = -1.0e30


class Chain:

    def __init__(self, eng, sem):
        self.eng, self.sem, self.n = eng, sem, 0

    def link(self, ins):
        ins.then_inc(self.sem, 1)
        self.n += 1
        self.eng.wait_ge(self.sem, self.n)


def hybrid_trunk(nc, x, a_w_in, a_conv, a_w_out, kv_w, b_w_q, b_w_o, ffn_w_gate, ffn_w_up, ffn_w_down,
                 moe_w_router, moe_w_gate, moe_w_up, moe_w_down, ln_g, ln_b, tables, out):
    _, SEQ, D = x.shape
    DEPTH = ln_g.shape[0]
    ALPHA = (2.0 * DEPTH) ** 0.25
    EPS = 1e-5
    F = ffn_w_gate.shape[2]
    E = moe_w_gate.shape[1]
    FE = moe_w_gate.shape[3]
    CW = a_conv.shape[1]
    AW = b_w_o.shape[1]
    HD = 64
    H = AW // HD
    NG = b_w_q.shape[2] // AW
    TT = SEQ // P
    KD = D // P
    HALF = D // BANK
    CH = 512
    CT = CH // P
    QI = 256
    assert TT == 2 and KD == 8 and HALF == 2 and CW == 3 and H == 8 and NG == 3 and E == 8
    assert KD * QI == ITEM and 2 * D == ITEM
    NCA = D // CH
    NFULL = F // CH
    assert F - NFULL * CH == QI
    NC = FE // CH
    assert NC * CH == FE and NC % 2 == 1
    PER_EXPERT = 6 * NC
    assert PER_EXPERT % RING == 0
    SCALE = HD ** -0.5

    with ExitStack() as ctx:
        def sb(name, shape, dt=F32):
            return ctx.enter_context(nc.sbuf_tensor(name, shape, dt))

        def sem(name):
            return ctx.enter_context(nc.semaphore(name))

        ring = sb("ring", [P, RING, ITEM])
        tok = sb("tok", [P, TT, D])
        chan = sb("chan", [P, KD, SEQ])
        res = sb("res", [P, TT, D])
        gb = sb("gb", [P, 2, D])
        tab = sb("tab", [P, 9, P])
        prow = sb("prow", [P, P])
        pcol = sb("pcol", [P, P])
        zero = sb("zero", [P, BANK], BF16)
        ones = sb("ones", [P, P])
        wr = sb("wr", [P, KD, E])
        flag = sb("flag", [P, 1], I32)
        stats = sb("stats", [P, TT, HALF, 6])
        mv = sb("mv", [P, TT, 4])
        soft = sb("soft", [P, 2, 4])
        lg = sb("lg", [P, TT, E])
        pr = sb("pr", [P, TT, E])
        prio = sb("prio", [P, E])
        hot = sb("hot", [P, 2, TT, E])
        top = sb("top", [P, 2, TT])
        pm = sb("pm", [P, TT])
        gate2 = sb("gate2", [P, 4, TT])
        sel = sb("sel", [P, E + 1, TT])
        comb = sb("comb", [P, E + 1, TT])
        rank = sb("rank", [P, E + 1, TT])
        peak = sb("peak", [P, 1])
        masked = sb("masked", [P, 2, NG * SEQ])
        probT = sb("probT", [P, 2, NG * SEQ])
        attT = sb("attT", [P, H // 2, SEQ])
        arena = sb("arena", [P, 9216])

        cut = [0]

        def view(size, fresh=False):
            if fresh:
                cut[0] = 0
            a = arena[:, cut[0]:cut[0] + size]
            cut[0] += size
            assert cut[0] <= 9216
            return a

        UPAD = SEQ + CW - 1
        gateB = view(CT * SEQ, True).rearrange("p (c t) -> p c t", c=CT)
        gateC = view(CT * SEQ).rearrange("p (c t) -> p c t", c=CT)
        upad = view(CT * UPAD).rearrange("p (c t) -> p c t", c=CT)
        conv = view(CT * SEQ).rearrange("p (c t) -> p c t", c=CT)
        mixT = view(KD * SEQ).rearrange("p (c t) -> p c t", c=KD)
        sgd = view(CT * SEQ)
        hidT = view(CT * SEQ, True).rearrange("p (c t) -> p c t", c=CT)
        NQ = NG * AW // P
        keyT = view(NQ * SEQ, True).rearrange("p (c t) -> p c t", c=NQ)
        qryT = view(NQ * SEQ).rearrange("p (c t) -> p c t", c=NQ)
        val = view(TT * NG * AW).rearrange("p (t n) -> p t n", t=TT)
        pick = view(SEQ, True).rearrange("p (t s) -> p t s", t=TT)
        back = view(SEQ)
        xe = view(KD * P).rearrange("p (k s) -> p k s", k=KD)
        sg = view(2 * CH).rearrange("p (b n) -> p b n", b=2)
        hid = view(CH)
        hT = view(2 * CH).rearrange("p (b n) -> p b n", b=2)
        ye = view(D)
        wsel = view(SEQ).rearrange("p (t s) -> p t s", t=TT)

        masks = tab[:, 0:6, :].rearrange("p (g k) s -> p g k s", k=2)
        ident = tab[:, 6, :]
        tri = tab[:, 7, :]
        slots = tab[:, 8, :]

        ps = ctx.enter_context(nc.psum_tensor("ps", [P, 8, BANK], F32))

        def banks(a, n):
            return ps[:, a:a + n, :].rearrange("p b n -> p (b n)")

        landed = [sem(f"landed{i}") for i in range(RING)]
        pieces = sem("pieces")
        x_in, tab_in, par_in, gb_in, wr_in = (sem(n) for n in ("x_in", "tab_in", "par_in", "gb_in", "wr_in"))
        const_set = sem("const_set")
        dve_steps = sem("dve_steps")
        par_t, par_done = sem("par_t"), sem("par_done")
        conv_ok = sem("conv_ok")
        rank_ok = sem("rank_ok")
        xT_ps = sem("xT_ps")
        xT_a, xT_d = sem("xT_act"), sem("xT_dve")
        gate_sb = sem("gate_sb")
        u_read = sem("u_read")
        mixT_ok = sem("mixT_ok")
        res_ok = sem("res_ok")
        var_ok, dev_ok = sem("var_ok"), sem("dev_ok")
        norm_ok = sem("norm_ok")
        tok_ok = sem("tok_ok")
        silu_ok, hid_ok = sem("silu_ok"), sem("hid_ok")
        kq_ok, v_ok = sem("kq_ok"), sem("v_ok")
        sc_ps = sem("sc_ps")
        max_ok = sem("max_ok")
        exp_ok = sem("exp_ok")
        prob_ok = sem("prob_ok")
        pT_ps, pT_ok = sem("pT_ps"), sem("pT_ok")
        o_ps, o_ok = sem("o_ps"), sem("o_ok")
        log_ps, rank_ps = sem("log_ps"), sem("rank_ps")
        lgap_ok, lexp_ok = sem("lgap_ok"), sem("lexp_ok")
        sel_ok = sem("sel_ok")
        flag_ok = sem("flag_ok")
        pick_ok = sem("pick_ok")
        wsel_ok = sem("wsel_ok")
        wT_ps, wT_ok = sem("wT_ps"), sem("wT_ok")
        acc_ok = sem("acc_ok")
        xe_ps, xe_ok = sem("xe_ps"), sem("xe_ok")
        esilu, ehid = sem("esilu"), sem("ehid")
        ht_ps, ht_ok = sem("ht_ps"), sem("ht_ok")
        ye_ok = sem("ye_ok")
        comb_ps, comb_ok = sem("comb_ps"), sem("comb_ok")
        fin_ok, stored = sem("fin_ok"), sem("stored")
        block = ctx.enter_context(nc.Block())

        x_d = x[0].rearrange("(t p) d -> p t d", p=P)
        out_d = out[0].rearrange("(t p) d -> p t d", p=P)

        def cols(w, c0):
            return w.rearrange("(k p) n -> p k n", p=P)[:, :, bass.ds(c0, QI)]

        def rows(w, r0):
            return w[bass.ds(r0, 2 * P), :].rearrange("(i p) d -> p i d", p=P)

        def as_cols(s):
            return ring[:, s, :].rearrange("p (k n) -> p k n", k=KD)

        def as_rows(s):
            return ring[:, s, :].rearrange("p (i n) -> p i n", i=2)

        slot_uses = [0] * RING
        slot_last = [-1] * RING
        total = [0]

        class Phase:
            def __init__(self, slot_list, rounds=1):
                self.start, self.slots, self.per = total[0], slot_list, len(slot_list)
                self.before = {s: slot_uses[s] for s in slot_list}
                self.last = {s: slot_last[s] for s in slot_list}
                self.turns = {s: slot_list.count(s) for s in slot_list}
                for s in slot_list * rounds:
                    slot_uses[s] += 1
                    slot_last[s] = total[0]
                    total[0] += 1

            def done(self, k, rnd=0):
                return rnd * self.per + (self.start + k)

            def landed(self, k, rnd=0):
                s = self.slots[k]
                turn = self.slots[:k].count(s)
                return rnd * (16 * self.turns[s]) + 16 * (self.before[s] + turn + 1)

            def free(self, k, rnd=0):
                s = self.slots[k]
                if s in self.slots[:k]:
                    back = k - max(n for n in range(k) if self.slots[n] == s)
                elif isinstance(rnd, int) and rnd == 0:
                    return self.last[s] + 1
                else:
                    back = k + self.per - max(n for n in range(self.per) if self.slots[n] == s)
                    if not isinstance(rnd, int):
                        back -= max(0, self.last[s] - (self.start + k - back))
                return rnd * self.per + (self.start + k - back + 1)

        conv_w = Phase([0, 1, 2, 3, 4, 5], NCA)
        conv_o = Phase([6, 7, 8, 9])
        dense_0 = Phase([10, 11])
        dense_w = Phase([2, 3, 10, 11, 0, 1], NFULL - 1)
        dense_z = Phase([2, 3, 4, 0, 1, 5, 13])
        qkv_w = Phase([6, 7, 8, 9, 10, 11], NG)
        att_o = Phase([12, 13])
        ORDER = [("gate", 0), ("up", 0)]
        for c in range(1, NC):
            ORDER += [("gate", c), ("up", c), ("down", c - 1)]
        ORDER += [("down", NC - 1)]
        expert_w = Phase([n % RING for n in range(PER_EXPERT)], 2 * E)
        AT = {what: 2 * n for n, what in enumerate(ORDER)}

        @block.sync
        def _(sp):
            def load(phase, k, view_, src, rnd=0):
                free = phase.free(k, rnd)
                if not isinstance(free, int) or free > 0:
                    sp.wait_ge(pieces, free)
                s = phase.slots[k]
                sp.dma_start(view_(s), src).then_inc(landed[s], 16)

            for i in range(NCA):
                for part in range(3):
                    for q in range(2):
                        load(conv_w, 2 * part + q, as_cols, cols(a_w_in[0], part * D + i * CH + q * QI), i)
            for q in range(4):
                load(conv_o, q, as_rows, rows(a_w_out[0], q * 2 * P))
            for q in range(2):
                load(dense_0, q, as_cols, cols(ffn_w_gate[0], q * QI))
            with sp.Fori(0, NFULL - 1) as i:
                for q in range(2):
                    load(dense_w, q, as_cols, cols(ffn_w_up[0], i * CH + q * QI), i)
                for q in range(2):
                    load(dense_w, 2 + q, as_cols, cols(ffn_w_gate[0], i * CH + (CH + q * QI)), i)
                for q in range(2):
                    load(dense_w, 4 + q, as_rows, rows(ffn_w_down[0], i * CH + q * 2 * P), i)
            i = NFULL - 1
            for q in range(2):
                load(dense_z, q, as_cols, cols(ffn_w_up[0], i * CH + q * QI))
            load(dense_z, 2, as_cols, cols(ffn_w_gate[0], NFULL * CH))
            for q in range(2):
                load(dense_z, 3 + q, as_rows, rows(ffn_w_down[0], i * CH + q * 2 * P))
            load(dense_z, 5, as_cols, cols(ffn_w_up[0], NFULL * CH))
            load(dense_z, 6, as_rows, rows(ffn_w_down[0], NFULL * CH))
            with sp.Fori(0, NG) as g:
                for q in range(2):
                    load(qkv_w, q, as_cols, cols(kv_w, g * (2 * AW) + q * QI), g)
                for q in range(2):
                    load(qkv_w, 2 + q, as_cols, cols(b_w_q[0], g * AW + q * QI), g)
                for q in range(2):
                    load(qkv_w, 4 + q, as_cols, cols(kv_w, g * (2 * AW) + (AW + q * QI)), g)
            for q in range(2):
                load(att_o, q, as_rows, rows(b_w_o[0], q * 2 * P))

            def expert(j, e):
                wg, wu, wd = (w[0][bass.ds(e, 1)].rearrange("o a b -> (o a) b") for w in (moe_w_gate, moe_w_up, moe_w_down))
                for n, (part, c) in enumerate(ORDER):
                    for q in range(2):
                        if part == "down":
                            load(expert_w, 2 * n + q, as_rows, rows(wd, c * CH + q * 2 * P), j)
                        else:
                            load(expert_w, 2 * n + q, as_cols, cols(wg if part == "gate" else wu, c * CH + q * QI), j)

            with sp.Fori(0, E) as j:
                expert(j, j)
            sp.wait_ge(flag_ok, 1)
            over = sp.value_load(flag[0:1, 0:1], min_val=0, max_val=1)
            with sp.If(over > 0):
                with sp.Fori(E, 2 * E) as j:
                    expert(j, j - E)
            with sp.Else():
                sp.nop()
            for t in range(TT):
                sp.wait_ge(fin_ok, t + 1)
                sp.dma_start(out_d[:, t, :], res[:, t, :]).then_inc(stored, 16)
            sp.wait_ge(stored, 16 * TT)

        @block.gpsimd
        def _(pool):
            pool.dma_start(tok[:], x_d).then_inc(x_in, 16)
            pool.dma_start(tab[:], tables.rearrange("n p s -> p n s")).then_inc(tab_in, 16)
            pool.memset(prow[:], 0.0).then_inc(const_set, 1)
            pool.memset(zero[:], 0.0).then_inc(const_set, 1)
            pool.memset(ones[:], 1.0).then_inc(const_set, 1)
            pool.wait_ge(const_set, 1)
            pool.dma_start(prow[0:4 * KD, :], ln_g.rearrange("l n (k p) -> (l n k) p", p=P)).then_inc(par_in, 16)
            pool.dma_start(prow[4 * KD:8 * KD, :], ln_b.rearrange("l n (k p) -> (l n k) p", p=P)).then_inc(par_in, 16)
            pool.dma_start(prow[8 * KD:(8 + CW) * KD, :], a_conv[0].rearrange("w (k p) -> (w k) p", p=P)).then_inc(par_in, 16)
            pool.dma_start(wr[:], moe_w_router[0].rearrange("(k p) e -> p k e", p=P)).then_inc(wr_in, 16)
            for n in range(4):
                if n:
                    pool.wait_ge(tok_ok, 2 * n)
                for v, vec in enumerate((ln_g, ln_b)):
                    pool.dma_start(gb[:, v, :], vec[n // 2, n % 2:n % 2 + 1, :].to_broadcast([P, D])).then_inc(gb_in, 16)
                if n == 3:
                    break
                pool.wait_ge(gb_in, 32 * (n + 1))
                pool.wait_ge(xT_ps, n + 2)
                for v, op in enumerate((ALU.mult, ALU.add)):
                    if v:
                        pool.wait_ge(tok_ok, 2 * n + 1)
                    pool.tensor_tensor(tok[:], tok[:], gb[:, v:v + 1, :].to_broadcast([P, TT, D]), op).then_inc(tok_ok, 1)

        @block.tensor
        def _(pe):
            def piece(phase, k, rnd=0):
                pe.wait_ge(landed[phase.slots[k]], phase.landed(k, rnd))
                return phase.slots[k]

            def turn_stream():
                for t in range(TT):
                    for k in range(KD):
                        last = pe.transpose(banks(2, 4)[:, k * SEQ + t * P:k * SEQ + (t + 1) * P],
                                            tok[:, t, k * P:(k + 1) * P], ident)
                return last

            def chan_cols(bank, slot_list, moving):
                for q, s in enumerate(slot_list):
                    w = as_cols(s)
                    for i in range(QI // P):
                        o = banks(bank, 2)[:, (2 * q + i) * SEQ:(2 * q + i + 1) * SEQ]
                        for k in range(KD):
                            last = pe.matmul(o, w[:, k, i * P:(i + 1) * P], moving[:, k, :],
                                             start=(k == 0), stop=(k == KD - 1))
                    last.then_inc(pieces, 1)

            def tok_rows(bank, slot_list, stationary, start, stop):
                for q, s in enumerate(slot_list):
                    for i in range(2):
                        c = 2 * q + i
                        for t in range(TT):
                            for h in range(HALF):
                                last = pe.matmul(ps[:, bank + 2 * t + h, :], stationary[:, c, t * P:(t + 1) * P],
                                                 as_rows(s)[:, i, h * BANK:(h + 1) * BANK],
                                                 start=start and q == 0 and i == 0,
                                                 stop=stop and s == slot_list[-1] and i == 1)
                    last.then_inc(pieces, 1)

            pe.wait_ge(tab_in, 16)
            pe.wait_ge(par_in, 48)
            pe.wait_ge(const_set, 3)
            pe.transpose(ps[:, 0, 0:P], prow[:], ident).then_inc(par_t, 1)
            pe.wait_ge(x_in, 16)
            turn_stream().then_inc(xT_ps, 1)

            pe.wait_ge(par_done, 1)
            pe.wait_ge(xT_a, 1)
            pe.wait_ge(xT_d, 1)
            with pe.Fori(0, NCA) as i:
                for part, bank in enumerate((0, 6, 2)):
                    chan_cols(bank, [piece(conv_w, 2 * part + q, i) for q in range(2)], chan)
                pe.wait_ge(gate_sb, i * 2 + 2)
                pe.wait_ge(u_read, i + 1)
            pe.wait_ge(mixT_ok, NCA + 1)
            tok_rows(0, [piece(conv_o, q) for q in range(4)], mixT, True, True)

            def after_norm(n):
                pe.wait_ge(norm_ok, TT * (n + 1))
                turn_stream().then_inc(xT_ps, 1)
                pe.wait_ge(xT_a, n + 2)
                pe.wait_ge(xT_d, n + 2)

            after_norm(0)

            for b in range(4):
                pe.matmul(ps[:, 4 + b, :], zero[:, 0:P], zero[:], start=True, stop=False)
            chan_cols(0, [piece(dense_0, q) for q in range(2)], chan)
            with pe.Fori(0, NFULL - 1) as i:
                chan_cols(2, [piece(dense_w, q, i) for q in range(2)], chan)
                pe.wait_ge(silu_ok, i + 1)
                chan_cols(0, [piece(dense_w, 2 + q, i) for q in range(2)], chan)
                pe.wait_ge(hid_ok, i + 1)
                tok_rows(4, [piece(dense_w, 4 + q, i) for q in range(2)], hidT, False, False)
            chan_cols(2, [piece(dense_z, q) for q in range(2)], chan)
            pe.wait_ge(silu_ok, NFULL)
            chan_cols(0, [piece(dense_z, 2)], chan)
            pe.wait_ge(hid_ok, NFULL)
            tok_rows(4, [piece(dense_z, 3 + q) for q in range(2)], hidT, False, False)
            chan_cols(2, [piece(dense_z, 5)], chan)
            pe.wait_ge(hid_ok, NFULL + 1)
            tok_rows(4, [piece(dense_z, 6)], hidT, False, True)
            after_norm(1)

            with pe.Fori(0, NG) as g:
                chan_cols(0, [piece(qkv_w, q, g) for q in range(2)], chan)
                chan_cols(2, [piece(qkv_w, 2 + q, g) for q in range(2)], chan)
                for q in range(2):
                    w = as_cols(piece(qkv_w, 4 + q, g))
                    for t in range(TT):
                        for k in range(KD):
                            last = pe.matmul(ps[:, 4 + t, q * QI:(q + 1) * QI], chan[:, k, t * P:(t + 1) * P],
                                             w[:, k, :], start=(k == 0), stop=(k == KD - 1), skip_group_check=True)
                    last.then_inc(pieces, 1)
                pe.wait_ge(kq_ok, g * 2 + 2)
                pe.wait_ge(v_ok, g + 1)

            units = [(pair, t, h) for pair in range(H // 2) for t in range(TT) for h in range(2)]

            def scores(n):
                pair, t, h = units[n]
                r = slice(HD * h, HD * h + HD)
                if n >= 2:
                    pe.wait_ge(max_ok, n - 1)
                w = (t + 1) * P
                o = banks(2 * (n % 2), 2).rearrange("p (g k) -> p g k", k=SEQ)
                for g in range(NG):
                    c = g * (AW // P) + pair
                    last = pe.matmul(o[:, g, 0:w], qryT[r, c, t * P:(t + 1) * P], keyT[r, c, 0:w], start=True, stop=True)
                last.then_inc(sc_ps, 1)

            def turn_probs(n):
                pair, t, h = units[n]
                pe.wait_ge(prob_ok, n + 1)
                if n >= 1:
                    pe.wait_ge(pT_ok, n)
                w = t + 1
                for g in range(NG):
                    for k in range(w):
                        m = g * w + k
                        last = pe.transpose(banks(4, 2)[:, m * P:(m + 1) * P], masked[:, n % 2, m * P:(m + 1) * P], ident)
                last.then_inc(pT_ps, 1)

            def outputs(n):
                pair, t, h = units[n]
                pe.wait_ge(pT_ok, n + 1)
                m = n // 2
                if h == 0 and m >= 2:
                    pe.wait_ge(o_ok, m - 1)
                w = t + 1
                for g in range(NG):
                    for k in range(w):
                        j = g * w + k
                        c = g * AW + (2 * pair + h) * HD
                        last = pe.matmul(ps[HD * h:HD * h + HD, 6 + m % 2, 0:P], val[:, k, c:c + HD],
                                         probT[:, n % 2, j * P:(j + 1) * P], start=(j == 0), stop=(j == NG * w - 1))
                last.then_inc(o_ps, 1)

            N = len(units)
            for n in range(N + 2):
                if n < N:
                    scores(n)
                if 1 <= n <= N:
                    turn_probs(n - 1)
                if n >= 2:
                    outputs(n - 2)
            pe.wait_ge(o_ok, H // 2 * TT)
            pe.wait_ge(max_ok, N)
            tok_rows(0, [piece(att_o, q) for q in range(2)], attT, True, True)
            after_norm(2)

            pe.wait_ge(wr_in, 16)
            for t in range(TT):
                for k in range(KD):
                    last = pe.matmul(ps[:, 0, t * E:(t + 1) * E], chan[:, k, t * P:(t + 1) * P], wr[:, k, :],
                                     start=(k == 0), stop=(k == KD - 1), skip_group_check=True)
            last.then_inc(log_ps, 1)
            pe.wait_ge(sel_ok, 1)
            pe.matmul(ps[:, 1, 0:E], tri, sel[:, 0:E, 0], start=True, stop=True, skip_group_check=True)
            pe.matmul(ps[:, 1, E:2 * E], tri, sel[:, 0:E, 1], start=True, stop=False, skip_group_check=True)
            pe.matmul(ps[:, 1, E:2 * E], ones[:], sel[:, 0:E, 0], start=False, stop=True, skip_group_check=True)
            pe.matmul(ps[:, 1, 2 * E:3 * E], ones[:], sel[:, 0:E, 0], start=True, stop=False, skip_group_check=True)
            pe.matmul(ps[:, 1, 2 * E:3 * E], ones[:], sel[:, 0:E, 1], start=False, stop=True,
                      skip_group_check=True).then_inc(rank_ps, 1)
            pe.wait_ge(tok_ok, 2 * 3)

            def gather():
                for k in range(KD):
                    for t in range(TT):
                        last = pe.matmul(banks(2, 2)[:, k * P:(k + 1) * P], tok[:, t, k * P:(k + 1) * P],
                                         pick[:, t, :], start=(t == 0), stop=(t == TT - 1),
                                         skip_group_check=True)
                last.then_inc(xe_ps, 1)

            def expert(j, rnd):
                def gate_up(c, part):
                    for q in range(2):
                        s = piece(expert_w, AT[("gate", "up")[part], c] + q, j)
                        for k in range(KD):
                            last = pe.matmul(ps[:, 2 * (c % 2) + part, q * QI:(q + 1) * QI], xe[:, k, :],
                                             as_cols(s)[:, k, :], start=(k == 0), stop=(k == KD - 1),
                                             skip_group_check=True)
                        last.then_inc(pieces, 1)

                def turn_hid(c):
                    pe.wait_ge(ehid, j * NC + c + 1)
                    for i in range(CT):
                        last = pe.transpose(ps[:, 6, i * P:(i + 1) * P], hid[:, i * P:(i + 1) * P], ident)
                    last.then_inc(ht_ps, 1)

                def down(c):
                    pe.wait_ge(ht_ok, j * NC + c + 1)
                    for q in range(2):
                        s = piece(expert_w, AT["down", c] + q, j)
                        for i in range(2):
                            n = 2 * q + i
                            for h in range(HALF):
                                last = pe.matmul(ps[:, 4 + h, :], hT[:, c % 2, n * P:(n + 1) * P],
                                                 as_rows(s)[:, i, h * BANK:(h + 1) * BANK],
                                                 start=(c == 0 and n == 0), stop=(c == NC - 1 and n == CT - 1))
                        last.then_inc(pieces, 1)

                pe.wait_ge(xe_ok, j * 2 + 2 * (1 + rnd))
                for c in range(NC):
                    if c == 1:
                        pe.wait_ge(comb_ok, j * 2 + 1)
                    gate_up(c, 0)
                    if c:
                        turn_hid(c - 1)
                    gate_up(c, 1)
                    if 0 < c < NC - 1:
                        down(c - 1)
                    if c == 2:
                        pe.wait_ge(wsel_ok, j + 1)
                        for t in range(TT):
                            last = pe.transpose(ps[:, 7, t * P:(t + 1) * P], wsel[:, t, :], ident)
                        last.then_inc(wT_ps, 1)
                pe.wait_ge(pick_ok, j + 2 + rnd)
                gather()
                turn_hid(NC - 1)
                down(NC - 2)
                down(NC - 1)
                pe.wait_ge(ye_ok, j * 2 + 2)
                pe.wait_ge(wT_ok, j + 1)
                pe.wait_ge(xe_ok, j * 2 + 2 * (2 + rnd))
                for t in range(TT):
                    for h in range(HALF):
                        last = pe.matmul(ps[:, 2 * t + h, :], back[:, t * P:(t + 1) * P], ye[:, h * BANK:(h + 1) * BANK],
                                         start=True, stop=True)
                    last.then_inc(comb_ps, 1)
                pe.wait_ge(comb_ok, j * 2 + 2)

            pe.wait_ge(pick_ok, 1)
            gather()
            with pe.Fori(0, E) as j:
                expert(j, 0)
            pe.wait_ge(flag_ok, 1)
            over = pe.value_load(flag[0:1, 0:1], min_val=0, max_val=1)
            with pe.If(over > 0):
                pe.wait_ge(pick_ok, E + 2)
                pe.wait_ge(comb_ok, 2 * E + 1)
                gather()
                with pe.Fori(E, 2 * E) as j:
                    expert(j, 1)
            with pe.Else():
                pe.nop()

        @block.scalar
        def _(act):
            G, B = 0, 4 * KD

            def chan_half(n):
                src = banks(4, 2).rearrange("p (k t) -> p k t", t=SEQ)
                if n == 0:
                    act.copy(chan[:, 4:8, :], src).then_inc(xT_a, 1)
                    return
                for k in range(4, 8):
                    last = act.activation(chan[:, k, :], src[:, k - 4, :], ACT.Identity,
                                          scale=pcol[:, G + (n - 1) * KD + k:G + (n - 1) * KD + k + 1],
                                          bias=pcol[:, B + (n - 1) * KD + k:B + (n - 1) * KD + k + 1])
                last.then_inc(xT_a, 1)

            def normalise(n):
                for t in range(TT):
                    act.wait_ge(var_ok, TT * n + t + 1)
                    act.activation(mv[:, t, 2:3], mv[:, t, 1:2], ACT.Sqrt).then_inc(dev_ok, 1)
                for t in range(TT):
                    act.wait_ge(res_ok, TT * n + t + 1)
                    act.activation(tok[:, t, :], res[:, t, :], ACT.Identity, scale=mv[:, t, 2:3],
                                   bias=mv[:, t, 3:4]).then_inc(norm_ok, 1)
                if n < 3:
                    act.wait_ge(xT_ps, n + 2)
                    chan_half(n + 1)

            act.wait_ge(xT_ps, 1)
            chan_half(0)
            with act.Fori(0, NCA) as i:
                act.wait_ge(pieces, conv_w.done(2, i))
                act.wait_ge(mixT_ok, i + 1)
                act.copy(gateB, banks(0, 2).rearrange("p (c t) -> p c t", c=CT)).then_inc(gate_sb, 1)
                act.wait_ge(pieces, conv_w.done(4, i))
                act.copy(gateC, banks(6, 2).rearrange("p (c t) -> p c t", c=CT)).then_inc(gate_sb, 1)
            normalise(0)

            def silu_dense(i, width, done):
                act.wait_ge(pieces, done)
                if not isinstance(i, int) or i > 0:
                    act.wait_ge(hid_ok, i)
                act.activation(sgd[:, 0:width], banks(0, 2)[:, 0:width], ACT.Silu).then_inc(silu_ok, 1)

            silu_dense(0, CT * SEQ, dense_0.done(2))
            with act.Fori(1, NFULL) as i:
                silu_dense(i, CT * SEQ, dense_w.done(4, i - 1))
            silu_dense(NFULL, QI // P * SEQ, dense_z.done(3))
            normalise(1)

            with act.Fori(0, NG) as g:
                act.wait_ge(pieces, qkv_w.done(2, g))
                act.copy(keyT[:, bass.ds(g * CT, CT), :], banks(0, 2).rearrange("p (c t) -> p c t", c=CT)).then_inc(kq_ok, 1)
                act.wait_ge(pieces, qkv_w.done(4, g))
                act.copy(qryT[:, bass.ds(g * CT, CT), :], banks(2, 2).rearrange("p (c t) -> p c t", c=CT)).then_inc(kq_ok, 1)

            def exp_unit(n):
                w = NG * ((n // 2 % 2) + 1) * P
                act.wait_ge(max_ok, n + 1)
                act.activation(masked[:, n % 2, 0:w], masked[:, n % 2, 0:w], ACT.Exp, scale=SCALE,
                               bias=soft[:, n % 2, 1:2], accum_out=soft[:, n % 2, 2:3]).then_inc(exp_ok, 1)

            def copy_probs(n):
                w = NG * ((n // 2 % 2) + 1) * P
                act.wait_ge(pT_ps, n + 1)
                if n >= 2:
                    act.wait_ge(o_ps, n - 1)
                act.copy(probT[:, n % 2, 0:w], banks(4, 2)[:, 0:w]).then_inc(pT_ok, 1)

            for n in range(TT * H + 1):
                if n < TT * H:
                    exp_unit(n)
                if n >= 1:
                    copy_probs(n - 1)
            normalise(2)

            act.wait_ge(lgap_ok, 1)
            act.activation(gate2[:, 1, :], gate2[:, 0, :], ACT.Exp).then_inc(lexp_ok, 1)

            def copy_xe():
                act.copy(xe[:, 0:4, :], ps[:, 2, :].rearrange("p (k s) -> p k s", k=4)).then_inc(xe_ok, 1)

            def expert(j, rnd):
                for c in range(NC):
                    act.wait_ge(pieces, expert_w.done(AT["gate", c] + 2, j))
                    act.activation(sg[:, c % 2, :], ps[:, 2 * (c % 2), :], ACT.Silu).then_inc(esilu, 1)
                    if c == 3:
                        act.wait_ge(wT_ps, j + 1)
                        act.copy(back, ps[:, 7, 0:SEQ]).then_inc(wT_ok, 1)
                act.wait_ge(xe_ps, j + 2 + rnd)
                copy_xe()
                act.wait_ge(pieces, expert_w.done(PER_EXPERT, j))
                act.copy(ye[:, 0:BANK], ps[:, 4, :]).then_inc(ye_ok, 1)

            act.wait_ge(xe_ps, 1)
            copy_xe()
            with act.Fori(0, E) as j:
                expert(j, 0)
            act.wait_ge(flag_ok, 1)
            over = act.value_load(flag[0:1, 0:1], min_val=0, max_val=1)
            with act.If(over > 0):
                act.wait_ge(xe_ps, E + 2)
                copy_xe()
                with act.Fori(E, 2 * E) as j:
                    expert(j, 1)
            with act.Else():
                act.nop()
            normalise(3)

        @block.vector
        def _(dve):
            chain = Chain(dve, dve_steps)
            G, B, C = 0, 4 * KD, 8 * KD

            def chan_half(n):
                dve.wait_ge(xT_ps, n + 1)
                src = banks(2, 2).rearrange("p (k t) -> p k t", t=SEQ)
                if n == 0:
                    dve.tensor_copy(chan[:, 0:4, :], src).then_inc(xT_d, 1)
                    return
                for k in range(4):
                    c = (n - 1) * KD + k
                    last = dve.tensor_scalar(chan[:, k, :], src[:, k, :], pcol[:, G + c:G + c + 1],
                                             pcol[:, B + c:B + c + 1], ALU.mult, ALU.add)
                last.then_inc(xT_d, 1)

            def statistics(t):
                for h in range(HALF):
                    last = dve.bn_stats(stats[:, t, h, :], res[:, t, h * BANK:(h + 1) * BANK])
                chain.link(last)
                chain.link(dve.bn_aggr(mv[:, t, 0:2], stats[:, t, :, :]))
                dve.tensor_scalar(mv[:, t, 1:2], mv[:, t, 1:2], EPS, None, ALU.add).then_inc(var_ok, 1)

            def scales(n, t):
                dve.wait_ge(dev_ok, TT * n + t + 1)
                chain.link(dve.reciprocal(mv[:, t, 2:3], mv[:, t, 2:3]))
                dve.tensor_scalar(mv[:, t, 3:4], mv[:, t, 0:1], mv[:, t, 2:3], -1.0, ALU.mult, ALU.mult).then_inc(res_ok, 1)

            def residual(n, bank, done):
                dve.wait_ge(pieces, done)
                if n:
                    dve.wait_ge(tok_ok, 2 * n)
                for t in range(TT):
                    chain.link(dve.scalar_tensor_tensor(out=res[:, t, :], in0=tok[:, t, :], scalar=ALPHA,
                                                        in1=banks(bank + 2 * t, 2), op0=ALU.mult, op1=ALU.add))
                    statistics(t)
                for t in range(TT):
                    scales(n, t)
                chan_half(n + 1)

            dve.memset(upad[:, :, 0:CW - 1], 0.0).then_inc(mixT_ok, 1)
            dve.wait_ge(par_t, 1)
            dve.tensor_copy(pcol[:], ps[:, 0, 0:P]).then_inc(par_done, 1)
            chan_half(0)

            def taps(w, i, c):
                return pcol[:, bass.ds(i * CT + (C + w * KD + c), 1)]

            with dve.Fori(0, NCA) as i:
                dve.wait_ge(pieces, conv_w.done(6, i))
                dve.wait_ge(gate_sb, i * 2 + 2)
                dve.tensor_tensor(upad[:, :, CW - 1:], banks(2, 2).rearrange("p (c t) -> p c t", c=CT), gateC,
                                  ALU.mult).then_inc(u_read, 1)
                dve.wait_ge(u_read, i + 1)
                for c in range(CT):
                    last = dve.tensor_scalar(conv[:, c, :], upad[:, c, 0:SEQ], taps(0, i, c), None, ALU.mult)
                last.then_inc(conv_ok, 1)
                for w in range(1, CW):
                    dve.wait_ge(conv_ok, i * CW + w)
                    for c in range(CT):
                        last = dve.scalar_tensor_tensor(out=conv[:, c, :], in0=upad[:, c, w:w + SEQ], scalar=taps(w, i, c),
                                                        in1=conv[:, c, :], op0=ALU.mult, op1=ALU.add)
                    last.then_inc(conv_ok, 1)
                dve.wait_ge(conv_ok, i * CW + CW)
                dve.tensor_tensor(mixT[:, bass.ds(i * CT, CT), :], conv, gateB, ALU.mult).then_inc(mixT_ok, 1)
            residual(0, 0, conv_o.done(4))

            def hidden(i, w, done):
                dve.wait_ge(silu_ok, i + 1)
                dve.wait_ge(pieces, done)
                dve.tensor_tensor(hidT.rearrange("p c t -> p (c t)")[:, 0:w], banks(2, 2)[:, 0:w], sgd[:, 0:w],
                                  ALU.mult).then_inc(hid_ok, 1)

            with dve.Fori(0, NFULL) as i:
                hidden(i, CT * SEQ, dense_w.done(2, i))
            hidden(NFULL, QI // P * SEQ, dense_z.done(6))
            residual(1, 4, dense_z.done(7))

            with dve.Fori(0, NG) as g:
                dve.wait_ge(pieces, qkv_w.done(6, g))
                dve.tensor_copy(val[:, :, bass.ds(g * AW, AW)], ps[:, 4:4 + TT, :]).then_inc(v_ok, 1)

            def maximum(n):
                t = n // 2 % 2
                w = (t + 1) * P
                dve.wait_ge(sc_ps, n + 1)
                if n >= 2:
                    dve.wait_ge(pT_ps, n - 1)
                src = banks(2 * (n % 2), 2)[:, 0:NG * SEQ].rearrange("p (g k) -> p g k", g=NG)[:, :, 0:w]
                m = (masks if t else masks[:, :, 1:2, :]).rearrange("p g k s -> p g (k s)") if t else masks[:, :, 1, :]
                dst = masked[:, n % 2, 0:NG * w].rearrange("p (g k) -> p g k", g=NG)
                chain.link(dve.tensor_tensor_reduce(out=dst, in0=src, in1=m, scale=1.0, scalar=-3.0e38,
                                                    op0=ALU.add, op1=ALU.max, accum_out=soft[:, n % 2, 0:1]))
                dve.tensor_scalar(soft[:, n % 2, 1:2], soft[:, n % 2, 0:1], -SCALE, None, ALU.mult).then_inc(max_ok, 1)

            def divide(n):
                w = NG * ((n // 2 % 2) + 1) * P
                dve.wait_ge(exp_ok, n + 1)
                chain.link(dve.reciprocal(soft[:, n % 2, 3:4], soft[:, n % 2, 2:3]))
                dve.tensor_scalar(masked[:, n % 2, 0:w], masked[:, n % 2, 0:w], soft[:, n % 2, 3:4], None,
                                  ALU.mult).then_inc(prob_ok, 1)

            def keep_outputs(m):
                dve.wait_ge(o_ps, 2 * m + 2)
                t = m % TT
                dve.tensor_copy(attT[:, m // TT, t * P:(t + 1) * P], ps[:, 6 + m % 2, 0:P]).then_inc(o_ok, 1)

            N = H * TT
            for n in range(N + 3):
                if n < N:
                    maximum(n)
                if 1 <= n <= N:
                    divide(n - 1)
                if n >= 3 and (n - 3) % 2 == 1:
                    keep_outputs((n - 3) // 2)
            residual(2, 0, att_o.done(2))

            dve.wait_ge(log_ps, 1)
            dve.tensor_copy(lg[:], ps[:, 0, 0:TT * E].rearrange("p (t e) -> p t e", t=TT))
            chain.link(dve.tensor_scalar(prio[:], slots[:, 0:E], -1.0, float(P), ALU.mult, ALU.add))
            for choice in range(2):
                chain.link(dve.tensor_reduce(top[:, choice, :], lg[:], AX_X, ALU.max))
                for t in range(TT):
                    last = dve.scalar_tensor_tensor(out=pr[:, t, :], in0=lg[:, t, :], scalar=top[:, choice, t:t + 1],
                                                    in1=prio[:], op0=ALU.is_equal, op1=ALU.mult)
                chain.link(last)
                chain.link(dve.tensor_reduce(pm[:], pr[:], AX_X, ALU.max))
                for t in range(TT):
                    last = dve.tensor_scalar(hot[:, choice, t, :], pr[:, t, :], pm[:, t:t + 1], None, ALU.is_equal)
                chain.link(last)
                if choice == 0:
                    chain.link(dve.scalar_tensor_tensor(out=lg[:], in0=hot[:, 0, :, :], scalar=-3.0e38, in1=lg[:],
                                                        op0=ALU.mult, op1=ALU.add))
            dve.tensor_tensor(gate2[:, 0, :], top[:, 1, :], top[:, 0, :], ALU.subtract).then_inc(lgap_ok, 1)
            dve.memset(sel[:, E:E + 1, :], 0.0)
            dve.memset(rank[:, E:E + 1, :], 0.0)
            dve.tensor_tensor(sel[:, 0:E, :], hot[:, 0, :, :].rearrange("p t e -> p e t"),
                              hot[:, 1, :, :].rearrange("p t e -> p e t"), ALU.add).then_inc(sel_ok, 1)
            dve.wait_ge(lexp_ok, 1)
            chain.link(dve.tensor_scalar(gate2[:, 3, :], gate2[:, 1, :], 1.0, None, ALU.add))
            chain.link(dve.reciprocal(gate2[:, 2, :], gate2[:, 3, :]))
            chain.link(dve.tensor_tensor(gate2[:, 3, :], gate2[:, 1, :], gate2[:, 2, :], ALU.mult))
            for t in range(TT):
                last = dve.tensor_scalar(comb[:, 0:E, t], hot[:, 0, t, :], gate2[:, 2, t:t + 1], None, ALU.mult)
            chain.link(last)
            for t in range(TT):
                dve.scalar_tensor_tensor(out=comb[:, 0:E, t], in0=hot[:, 1, t, :], scalar=gate2[:, 3, t:t + 1],
                                         in1=comb[:, 0:E, t], op0=ALU.mult, op1=ALU.add)
            dve.wait_ge(rank_ps, 1)
            chain.link(dve.tensor_copy(rank[:, 0:E, :], ps[:, 1, 0:TT * E].rearrange("p (t e) -> p e t", t=TT)))

            def picker(dst, e, values, done):
                for t in range(TT):
                    last = dve.tensor_scalar(dst[:, t, :], slots, rank[:, bass.ds(e, 1), t], values[:, bass.ds(e, 1), t],
                                             ALU.is_equal, ALU.mult)
                last.then_inc(done, 1)

            picker(pick, 0, sel, pick_ok)
            chain.link(dve.tensor_reduce(peak[:], ps[:, 1, 2 * E:3 * E], AX_X, ALU.max))
            chain.link(dve.tensor_scalar(flag[:], peak[:], float(P), None, ALU.is_gt))
            dve.wait_ge(tok_ok, 2 * 3)
            dve.tensor_scalar(res[:], tok[:], ALPHA, None, ALU.mult).then_inc(comb_ok, 1)
            dve.engine_nop().then_inc(flag_ok, 1)

            def copy_xe():
                dve.tensor_copy(xe[:, 4:8, :], ps[:, 3, :].rearrange("p (k s) -> p k s", k=4)).then_inc(xe_ok, 1)

            def expert(j, e, rnd):
                def copy_hid(c):
                    dve.wait_ge(ht_ps, j * NC + c + 1)
                    dve.tensor_copy(hT[:, c % 2, :], ps[:, 6, :]).then_inc(ht_ok, 1)

                picker(pick, e + 1, sel, pick_ok)
                picker(wsel, e, comb, wsel_ok)
                for c in range(NC):
                    if c:
                        copy_hid(c - 1)
                    dve.wait_ge(esilu, j * NC + c + 1)
                    dve.wait_ge(pieces, expert_w.done(AT["up", c] + 2, j))
                    dve.tensor_tensor(hid, ps[:, 2 * (c % 2) + 1, :], sg[:, c % 2, :], ALU.mult).then_inc(ehid, 1)
                dve.wait_ge(xe_ps, j + 2 + rnd)
                copy_xe()
                copy_hid(NC - 1)
                dve.wait_ge(pieces, expert_w.done(PER_EXPERT, j))
                dve.tensor_copy(ye[:, BANK:D], ps[:, 5, :]).then_inc(ye_ok, 1)
                for t in range(TT):
                    dve.wait_ge(comb_ps, j * 2 + t + 1)
                    dve.tensor_tensor(res[:, t, :], banks(2 * t, 2), res[:, t, :], ALU.add).then_inc(comb_ok, 1)
                dve.wait_ge(comb_ok, j * 2 + 3)

            dve.wait_ge(xe_ps, 1)
            copy_xe()
            with dve.Fori(0, E) as j:
                expert(j, j, 0)
            over = dve.value_load(flag[0:1, 0:1], min_val=0, max_val=1)
            with dve.If(over > 0):
                dve.tensor_scalar(rank[:], rank[:], -float(P), None, ALU.add).then_inc(rank_ok, 1)
                dve.wait_ge(rank_ok, 1)
                picker(pick, 0, sel, pick_ok)
                dve.wait_ge(xe_ps, E + 2)
                copy_xe()
                with dve.Fori(E, 2 * E) as j:
                    expert(j, j - E, 1)
            with dve.Else():
                dve.nop()
            for t in range(TT):
                statistics(t)
            for t in range(TT):
                scales(3, t)
            dve.wait_ge(gb_in, 32 * 4)
            for t in range(TT):
                dve.wait_ge(norm_ok, TT * 3 + t + 1)
                chain.link(dve.tensor_tensor(res[:, t, :], tok[:, t, :], gb[:, 0, :], ALU.mult))
                dve.tensor_tensor(res[:, t, :], res[:, t, :], gb[:, 1, :], ALU.add).then_inc(fin_ok, 1)


def launch_tables(P, window_spans):
    import numpy as np

    q = np.arange(P)[:, None]
    k = np.arange(P)[None, :]
    out = []
    for span, dil in window_spans:
        for back in (P, 0):
            dist = back + q - k
            ok = (dist >= 0) & (dist % dil == 0) & (dist <= span * dil)
            out.append(np.where(ok, 0.0, FAR))
    out.append(np.eye(P))
    out.append(q < k)
    out.append(np.broadcast_to(k, (P, P)))
    return np.stack([np.asarray(a, np.float32) for a in out])


_INS = ['x', 'a_w_in', 'a_conv', 'a_w_out', 'kv_w', 'b_w_q', 'b_w_o', 'ffn_w_gate', 'ffn_w_up', 'ffn_w_down',
        'moe_w_router', 'moe_w_gate', 'moe_w_up', 'moe_w_down', 'ln_g', 'ln_b']


def kernel(**inputs):
    import numpy as _np
    import concourse.bacc as _bacc
    from concourse import mybir as _mybir
    from concourse.bass_utils import run_bass_kernel_spmd as _run

    nc = _bacc.Bacc("TRN2", target_bir_lowering=False, num_devices=1)
    arrays, args = {}, []
    for name in _INS:
        a = _np.ascontiguousarray(inputs[name])
        arrays[f"in_{name}_dram"] = a
        args.append(nc.dram_tensor(f"in_{name}_dram", a.shape, _mybir.dt.from_np(a.dtype), kind="ExternalInput").ap())
    tables = launch_tables(128, ((128, 1), (128, 4), (128, 16)))
    arrays["tables_dram"] = tables
    args.append(nc.dram_tensor("tables_dram", tables.shape, _mybir.dt.float32, kind="ExternalInput").ap())
    args.append(nc.dram_tensor("out_0_dram", inputs["x"].shape, _mybir.dt.float32, kind="ExternalOutput").ap())
    hybrid_trunk(nc, *args)
    r = _run(nc, [arrays], core_ids=[0])
    return r.results[0]["out_0_dram"]
```

```python
from contextlib import ExitStack

import concourse.bass as bass
from concourse import mybir

F32 = mybir.dt.float32
F32R = mybir.dt.float32r
I32 = mybir.dt.int32
BF16 = mybir.dt.bfloat16
ALU = mybir.AluOpType
ACT = mybir.ActivationFunctionType
AX_X = mybir.AxisListType.X

P = 128
BANK = 512
ITEM = 2048
RAW = 6
SPLIT = 3
FAR = -1.0e30


class Chain:

    def __init__(self, eng, sem):
        self.eng, self.sem, self.n = eng, sem, 0

    def link(self, ins):
        ins.then_inc(self.sem, 1)
        self.n += 1
        self.eng.wait_ge(self.sem, self.n)


def hybrid_trunk(nc, x, a_w_in, a_conv, a_w_out, kv_w, b_w_q, b_w_o, ffn_w_gate, ffn_w_up, ffn_w_down,
                 moe_w_router, moe_w_gate, moe_w_up, moe_w_down, ln_g, ln_b, tables, out):
    _, SEQ, D = x.shape
    DEPTH = ln_g.shape[0]
    ALPHA = (2.0 * DEPTH) ** 0.25
    EPS = 1e-5
    F = ffn_w_gate.shape[2]
    E = moe_w_gate.shape[1]
    FE = moe_w_gate.shape[3]
    CW = a_conv.shape[1]
    AW = b_w_o.shape[1]
    HD = 64
    H = AW // HD
    NG = b_w_q.shape[2] // AW
    TT = SEQ // P
    KD = D // P
    HALF = D // BANK
    CH = 512
    CT = CH // P
    QI = 256
    assert TT == 2 and KD == 8 and HALF == 2 and CW == 3 and H == 8 and NG == 3 and E == 8
    assert KD * QI == ITEM and 2 * D == ITEM
    NCA = D // CH
    NFULL = F // CH
    assert F - NFULL * CH == QI
    NC = FE // CH
    assert NC * CH == FE and NC % 2 == 1
    PER_EXPERT = 6 * NC
    assert PER_EXPERT % RAW == 0 and RAW % SPLIT == 0
    SCALE = HD ** -0.5

    with ExitStack() as ctx:
        def sb(name, shape, dt=F32):
            return ctx.enter_context(nc.sbuf_tensor(name, shape, dt))

        def sem(name):
            return ctx.enter_context(nc.semaphore(name))

        raw = sb("raw", [P, RAW, ITEM])
        wh = sb("wh", [P, SPLIT, ITEM], F32R)
        wl = sb("wl", [P, SPLIT, ITEM], F32R)
        tok = sb("tok", [P, TT, D])
        chh = sb("chh", [P, KD, SEQ], F32R)
        chl = sb("chl", [P, KD, SEQ], F32R)
        parts = sb("parts", [P, 2, ITEM], F32R)
        res = sb("res", [P, TT, D])
        gb = sb("gb", [P, 2, D])
        tab = sb("tab", [P, 9, P])
        pcol = sb("pcol", [P, P])
        zero = sb("zero", [P, BANK], BF16)
        ones = sb("ones", [P, P])
        wr = sb("wr", [P, KD, E])
        flag = sb("flag", [P, 1], I32)
        stats = sb("stats", [P, TT, HALF, 6])
        mv = sb("mv", [P, TT, 4])
        soft = sb("soft", [P, 2, 4])
        lg = sb("lg", [P, TT, E])
        pr = sb("pr", [P, TT, E])
        prio = sb("prio", [P, E])
        hot = sb("hot", [P, 2, TT, E])
        top = sb("top", [P, 2, TT])
        pm = sb("pm", [P, TT])
        gate2 = sb("gate2", [P, 4, TT])
        sel = sb("sel", [P, E + 1, TT])
        comb = sb("comb", [P, E + 1, TT])
        rank = sb("rank", [P, E + 1, TT])
        peak = sb("peak", [P, 1])
        arena = sb("arena", [P, 12288])

        cut = [0]

        def view(size, fresh=False):
            if fresh:
                cut[0] = 0
            a = arena[:, cut[0]:cut[0] + size]
            cut[0] += size
            assert cut[0] <= 12288
            return a

        prow = arena[:, 12288 - P:]
        UPAD = SEQ + CW - 1
        gateB = view(CT * SEQ, True).rearrange("p (c t) -> p c t", c=CT)
        gateC = view(CT * SEQ).rearrange("p (c t) -> p c t", c=CT)
        upad = view(CT * UPAD).rearrange("p (c t) -> p c t", c=CT)
        conv = view(CT * SEQ).rearrange("p (c t) -> p c t", c=CT)
        mixh = parts[:, 0, :].rearrange("p (c t) -> p c t", c=KD)
        mixl = parts[:, 1, :].rearrange("p (c t) -> p c t", c=KD)
        chan = view(KD * SEQ, True).rearrange("p (c t) -> p c t", c=KD)
        sgd = view(CT * SEQ)
        hidh = parts[:, 0, 0:CT * SEQ].rearrange("p (c t) -> p c t", c=CT)
        hidl = parts[:, 1, 0:CT * SEQ].rearrange("p (c t) -> p c t", c=CT)
        NQ = NG * AW // P
        keyT = view(NQ * SEQ, True).rearrange("p (c t) -> p c t", c=NQ)
        qryT = view(NQ * SEQ).rearrange("p (c t) -> p c t", c=NQ)
        val = view(TT * NG * AW).rearrange("p (t n) -> p t n", t=TT)
        masked = view(2 * NG * SEQ).rearrange("p (b n) -> p b n", b=2)
        probT = view(2 * NG * SEQ).rearrange("p (b n) -> p b n", b=2)
        atth = parts[:, 0, 0:H // 2 * SEQ].rearrange("p (c t) -> p c t", c=H // 2)
        attl = parts[:, 1, 0:H // 2 * SEQ].rearrange("p (c t) -> p c t", c=H // 2)
        view(KD * SEQ, True)
        pick = view(SEQ).rearrange("p (t s) -> p t s", t=TT)
        back = view(SEQ)
        sg = view(2 * CH).rearrange("p (b n) -> p b n", b=2)
        hid = view(CH)
        ye = view(D)
        wsel = view(SEQ).rearrange("p (t s) -> p t s", t=TT)
        xeh = parts[:, 0, 0:KD * P].rearrange("p (k s) -> p k s", k=KD)
        xel = parts[:, 1, 0:KD * P].rearrange("p (k s) -> p k s", k=KD)
        hTh = parts[:, 0, KD * P:KD * P + 2 * CH].rearrange("p (b n) -> p b n", b=2)
        hTl = parts[:, 1, KD * P:KD * P + 2 * CH].rearrange("p (b n) -> p b n", b=2)

        masks = tab[:, 0:6, :].rearrange("p (g k) s -> p g k s", k=2)
        ident = tab[:, 6, :]
        tri = tab[:, 7, :]
        slots = tab[:, 8, :]

        ps = ctx.enter_context(nc.psum_tensor("ps", [P, 8, BANK], F32))

        def banks(a, n):
            return ps[:, a:a + n, :].rearrange("p b n -> p (b n)")

        landed = [sem(f"landed{i}") for i in range(RAW)]
        high_ok = sem("high_ok")
        low_ok = sem("low_ok")
        pieces = sem("pieces")
        x_in, tab_in, par_in, gb_in, wr_in = (sem(n) for n in ("x_in", "tab_in", "par_in", "gb_in", "wr_in"))
        const_set = sem("const_set")
        dve_steps = sem("dve_steps")
        par_t, par_done = sem("par_t"), sem("par_done")
        conv_ok = sem("conv_ok")
        rank_ok = sem("rank_ok")
        xT_ps = sem("xT_ps")
        chan_a, chan_d = sem("chan_act"), sem("chan_dve")
        ch_high, ch_low = sem("ch_high"), sem("ch_low")
        gate_sb = sem("gate_sb")
        u_read = sem("u_read")
        mixT_ok = sem("mixT_ok")
        res_ok = sem("res_ok")
        var_ok, dev_ok = sem("var_ok"), sem("dev_ok")
        norm_ok = sem("norm_ok")
        tok_ok = sem("tok_ok")
        silu_ok, hid_ok = sem("silu_ok"), sem("hid_ok")
        kq_ok, v_ok = sem("kq_ok"), sem("v_ok")
        sc_ps = sem("sc_ps")
        max_ok = sem("max_ok")
        exp_ok = sem("exp_ok")
        prob_ok = sem("prob_ok")
        pT_ps, pT_ok = sem("pT_ps"), sem("pT_ok")
        o_ps, o_ok = sem("o_ps"), sem("o_ok")
        log_ps, rank_ps = sem("log_ps"), sem("rank_ps")
        lgap_ok, lexp_ok = sem("lgap_ok"), sem("lexp_ok")
        sel_ok = sem("sel_ok")
        flag_ok = sem("flag_ok")
        pick_ok = sem("pick_ok")
        wsel_ok = sem("wsel_ok")
        wT_ps, wT_ok = sem("wT_ps"), sem("wT_ok")
        acc_ok = sem("acc_ok")
        xe_ps, xe_high, xe_ok = sem("xe_ps"), sem("xe_high"), sem("xe_ok")
        esilu, ehid = sem("esilu"), sem("ehid")
        ht_ps, ht_high, ht_ok = sem("ht_ps"), sem("ht_high"), sem("ht_ok")
        hsplit = sem("hsplit")
        msplit = sem("msplit")
        ye_ok = sem("ye_ok")
        comb_ps, comb_ok = sem("comb_ps"), sem("comb_ok")
        fin_ok, stored = sem("fin_ok"), sem("stored")
        block = ctx.enter_context(nc.Block())

        x_d = x[0].rearrange("(t p) d -> p t d", p=P)
        out_d = out[0].rearrange("(t p) d -> p t d", p=P)

        def cols(w, c0):
            return w.rearrange("(k p) n -> p k n", p=P)[:, :, bass.ds(c0, QI)]

        def rows(w, r0):
            return w[bass.ds(r0, 2 * P), :].rearrange("(i p) d -> p i d", p=P)

        def as_cols(a):
            return a.rearrange("p (k n) -> p k n", k=KD)

        def as_rows(a):
            return a.rearrange("p (i n) -> p i n", i=2)

        total = [0]

        class Phase:
            def __init__(self, per, rounds=1):
                self.start, self.per = total[0], per
                assert rounds == 1 or per % RAW == 0
                total[0] += per * rounds

            def done(self, k, rnd=0):
                return rnd * self.per + (self.start + k)

            def landed(self, k, rnd=0):
                return rnd * (16 * (self.per // RAW)) + 16 * ((self.start + k) // RAW + 1)

            def raw(self, k):
                return (self.start + k) % RAW

            def split(self, k):
                return (self.start + k) % SPLIT

        conv_w = Phase(6, NCA)
        conv_o = Phase(4)
        dense_0 = Phase(2)
        dense_w = Phase(6, NFULL - 1)
        dense_z = Phase(7)
        qkv_w = Phase(6, NG)
        att_o = Phase(2)
        ORDER = [("gate", 0), ("up", 0)]
        for c in range(1, NC):
            ORDER += [("gate", c), ("up", c), ("down", c - 1)]
        ORDER += [("down", NC - 1)]
        expert_w = Phase(PER_EXPERT, 2 * E)
        AT = {what: 2 * n for n, what in enumerate(ORDER)}

        @block.sync
        def _(sp):
            def load(phase, k, view_, src, rnd=0):
                if not isinstance(rnd, int) or phase.done(k, rnd) >= RAW:
                    sp.wait_ge(low_ok, phase.done(k + 1 - RAW, rnd))
                s = phase.raw(k)
                sp.dma_start(view_(raw[:, s, :]), src).then_inc(landed[s], 16)

            for i in range(NCA):
                for part in range(3):
                    for q in range(2):
                        load(conv_w, 2 * part + q, as_cols, cols(a_w_in[0], part * D + i * CH + q * QI), i)
            for q in range(4):
                load(conv_o, q, as_rows, rows(a_w_out[0], q * 2 * P))
            for q in range(2):
                load(dense_0, q, as_cols, cols(ffn_w_gate[0], q * QI))
            with sp.Fori(0, NFULL - 1) as i:
                for q in range(2):
                    load(dense_w, q, as_cols, cols(ffn_w_up[0], i * CH + q * QI), i)
                for q in range(2):
                    load(dense_w, 2 + q, as_cols, cols(ffn_w_gate[0], i * CH + (CH + q * QI)), i)
                for q in range(2):
                    load(dense_w, 4 + q, as_rows, rows(ffn_w_down[0], i * CH + q * 2 * P), i)
            i = NFULL - 1
            for q in range(2):
                load(dense_z, q, as_cols, cols(ffn_w_up[0], i * CH + q * QI))
            load(dense_z, 2, as_cols, cols(ffn_w_gate[0], NFULL * CH))
            for q in range(2):
                load(dense_z, 3 + q, as_rows, rows(ffn_w_down[0], i * CH + q * 2 * P))
            load(dense_z, 5, as_cols, cols(ffn_w_up[0], NFULL * CH))
            load(dense_z, 6, as_rows, rows(ffn_w_down[0], NFULL * CH))
            with sp.Fori(0, NG) as g:
                for q in range(2):
                    load(qkv_w, q, as_cols, cols(kv_w, g * (2 * AW) + q * QI), g)
                for q in range(2):
                    load(qkv_w, 2 + q, as_cols, cols(b_w_q[0], g * AW + q * QI), g)
                for q in range(2):
                    load(qkv_w, 4 + q, as_cols, cols(kv_w, g * (2 * AW) + (AW + q * QI)), g)
            for q in range(2):
                load(att_o, q, as_rows, rows(b_w_o[0], q * 2 * P))

            def expert(j, e):
                wg, wu, wd = (w[0][bass.ds(e, 1)].rearrange("o a b -> (o a) b") for w in (moe_w_gate, moe_w_up, moe_w_down))
                for n, (part, c) in enumerate(ORDER):
                    for q in range(2):
                        if part == "down":
                            load(expert_w, 2 * n + q, as_rows, rows(wd, c * CH + q * 2 * P), j)
                        else:
                            load(expert_w, 2 * n + q, as_cols, cols(wg if part == "gate" else wu, c * CH + q * QI), j)

            with sp.Fori(0, E) as j:
                expert(j, j)
            sp.wait_ge(flag_ok, 1)
            over = sp.value_load(flag[0:1, 0:1], min_val=0, max_val=1)
            with sp.If(over > 0):
                with sp.Fori(E, 2 * E) as j:
                    expert(j, j - E)
            with sp.Else():
                sp.nop()
            for t in range(TT):
                sp.wait_ge(fin_ok, t + 1)
                sp.dma_start(out_d[:, t, :], res[:, t, :]).then_inc(stored, 16)
            sp.wait_ge(stored, 16 * TT)

        @block.gpsimd
        def _(pool):
            pool.dma_start(tok[:], x_d).then_inc(x_in, 16)
            pool.dma_start(tab[:], tables.rearrange("n p s -> p n s")).then_inc(tab_in, 16)
            pool.memset(prow, 0.0).then_inc(const_set, 1)
            pool.memset(zero[:], 0.0).then_inc(const_set, 1)
            pool.memset(ones[:], 1.0).then_inc(const_set, 1)
            pool.wait_ge(const_set, 1)
            pool.dma_start(prow[0:4 * KD, :], ln_g.rearrange("l n (k p) -> (l n k) p", p=P)).then_inc(par_in, 16)
            pool.dma_start(prow[4 * KD:8 * KD, :], ln_b.rearrange("l n (k p) -> (l n k) p", p=P)).then_inc(par_in, 16)
            pool.dma_start(prow[8 * KD:(8 + CW) * KD, :], a_conv[0].rearrange("w (k p) -> (w k) p", p=P)).then_inc(par_in, 16)
            pool.dma_start(wr[:], moe_w_router[0].rearrange("(k p) e -> p k e", p=P)).then_inc(wr_in, 16)
            for n in range(4):
                if n:
                    pool.wait_ge(tok_ok, 2 * n)
                for v, vec in enumerate((ln_g, ln_b)):
                    pool.dma_start(gb[:, v, :], vec[n // 2, n % 2:n % 2 + 1, :].to_broadcast([P, D])).then_inc(gb_in, 16)
                if n == 3:
                    break
                pool.wait_ge(gb_in, 32 * (n + 1))
                pool.wait_ge(xT_ps, n + 2)
                for v, op in enumerate((ALU.mult, ALU.add)):
                    if v:
                        pool.wait_ge(tok_ok, 2 * n + 1)
                    pool.tensor_tensor(tok[:], tok[:], gb[:, v:v + 1, :].to_broadcast([P, TT, D]), op).then_inc(tok_ok, 1)

        @block.tensor
        def _(pe):
            def piece(phase, k, rnd=0):
                pe.wait_ge(low_ok, phase.done(k + 1, rnd))
                s = phase.split(k)
                return wh[:, s, :], wl[:, s, :]

            def product(out, stationary, moving, start, stop):
                sh, sl = stationary
                mh, ml = moving
                pe.matmul(out, sh, mh, start=start, stop=False)
                pe.matmul(out, sh, ml, start=False, stop=False)
                return pe.matmul(out, sl, mh, start=False, stop=stop)

            def turn_stream():
                for t in range(TT):
                    for k in range(KD):
                        last = pe.transpose(banks(2, 4)[:, k * SEQ + t * P:k * SEQ + (t + 1) * P],
                                            tok[:, t, k * P:(k + 1) * P], ident)
                return last

            def chan_cols(bank, phase, places, rnd=0):
                for q, n in enumerate(places):
                    hi, lo = (as_cols(w) for w in piece(phase, n, rnd))
                    for i in range(QI // P):
                        o = banks(bank, 2)[:, (2 * q + i) * SEQ:(2 * q + i + 1) * SEQ]
                        c = slice(i * P, (i + 1) * P)
                        for k in range(KD):
                            last = product(o, (hi[:, k, c], lo[:, k, c]), (chh[:, k, :], chl[:, k, :]),
                                           k == 0, k == KD - 1)
                    last.then_inc(pieces, 1)

            def tok_rows(bank, phase, places, stationary, start, stop, rnd=0, first=0):
                for q, n in enumerate(places):
                    hi, lo = (as_rows(w) for w in piece(phase, n, rnd))
                    for i in range(2):
                        c = first + 2 * q + i
                        for t in range(TT):
                            rows_t = slice(t * P, (t + 1) * P)
                            for h in range(HALF):
                                cols_h = slice(h * BANK, (h + 1) * BANK)
                                last = product(ps[:, bank + 2 * t + h, :],
                                               [a[:, c, rows_t] for a in stationary],
                                               (hi[:, i, cols_h], lo[:, i, cols_h]),
                                               start and q == 0 and i == 0, stop and n == places[-1] and i == 1)
                    last.then_inc(pieces, 1)

            pe.wait_ge(tab_in, 16)
            pe.wait_ge(par_in, 48)
            pe.wait_ge(const_set, 3)
            pe.transpose(ps[:, 0, 0:P], prow, ident).then_inc(par_t, 1)
            pe.wait_ge(x_in, 16)
            turn_stream().then_inc(xT_ps, 1)

            pe.wait_ge(par_done, 1)
            pe.wait_ge(ch_low, 2)
            with pe.Fori(0, NCA) as i:
                for part, bank in enumerate((0, 6, 2)):
                    chan_cols(bank, conv_w, (2 * part, 2 * part + 1), i)
                pe.wait_ge(gate_sb, i * 2 + 2)
                pe.wait_ge(u_read, i + 1)
            for i in range(NCA):
                pe.wait_ge(mixT_ok, i + 2)
                tok_rows(4, conv_o, (2 * i, 2 * i + 1), (mixh, mixl), i == 0, i == NCA - 1, first=i * CT)

            def after_norm(n):
                pe.wait_ge(norm_ok, TT * (n + 1))
                turn_stream().then_inc(xT_ps, 1)
                pe.wait_ge(ch_low, 2 * (n + 2))

            after_norm(0)

            for b in range(4):
                pe.matmul(ps[:, 4 + b, :], zero[:, 0:P], zero[:], start=True, stop=False)
            chan_cols(0, dense_0, (0, 1))
            hidT = (hidh, hidl)
            with pe.Fori(0, NFULL - 1) as i:
                chan_cols(2, dense_w, (0, 1), i)
                pe.wait_ge(silu_ok, i + 1)
                chan_cols(0, dense_w, (2, 3), i)
                pe.wait_ge(hid_ok, i + 1)
                tok_rows(4, dense_w, (4, 5), hidT, False, False, i)
            chan_cols(2, dense_z, (0, 1))
            pe.wait_ge(silu_ok, NFULL)
            chan_cols(0, dense_z, (2,))
            pe.wait_ge(hid_ok, NFULL)
            tok_rows(4, dense_z, (3, 4), hidT, False, False)
            chan_cols(2, dense_z, (5,))
            pe.wait_ge(hid_ok, NFULL + 1)
            tok_rows(4, dense_z, (6,), hidT, False, True)
            after_norm(1)

            with pe.Fori(0, NG) as g:
                chan_cols(0, qkv_w, (0, 1), g)
                chan_cols(2, qkv_w, (2, 3), g)
                pe.wait_ge(v_ok, g + 1)
                for q in range(2):
                    hi, lo = (as_cols(w) for w in piece(qkv_w, 4 + q, g))
                    for t in range(TT):
                        c = slice(t * P, (t + 1) * P)
                        for k in range(KD):
                            last = product(ps[:, 4 + t, q * QI:(q + 1) * QI], (chh[:, k, c], chl[:, k, c]),
                                           (hi[:, k, :], lo[:, k, :]), k == 0, k == KD - 1)
                    last.then_inc(pieces, 1)
                pe.wait_ge(kq_ok, g * 2 + 2)
            pe.wait_ge(v_ok, NG + 1)

            units = [(pair, t, h) for pair in range(H // 2) for t in range(TT) for h in range(2)]

            def scores(n):
                pair, t, h = units[n]
                r = slice(HD * h, HD * h + HD)
                if n >= 2:
                    pe.wait_ge(max_ok, n - 1)
                w = (t + 1) * P
                o = banks(2 * (n % 2), 2).rearrange("p (g k) -> p g k", k=SEQ)
                for g in range(NG):
                    c = g * (AW // P) + pair
                    last = pe.matmul(o[:, g, 0:w], qryT[r, c, t * P:(t + 1) * P], keyT[r, c, 0:w], start=True, stop=True)
                last.then_inc(sc_ps, 1)

            def turn_probs(n):
                pair, t, h = units[n]
                pe.wait_ge(prob_ok, n + 1)
                if n >= 1:
                    pe.wait_ge(pT_ok, n)
                w = t + 1
                for g in range(NG):
                    for k in range(w):
                        m = g * w + k
                        last = pe.transpose(banks(4, 2)[:, m * P:(m + 1) * P], masked[:, n % 2, m * P:(m + 1) * P], ident)
                last.then_inc(pT_ps, 1)

            def outputs(n):
                pair, t, h = units[n]
                pe.wait_ge(pT_ok, n + 1)
                m = n // 2
                if h == 0 and m >= 2:
                    pe.wait_ge(o_ok, m - 1)
                w = t + 1
                for g in range(NG):
                    for k in range(w):
                        j = g * w + k
                        c = g * AW + (2 * pair + h) * HD
                        last = pe.matmul(ps[HD * h:HD * h + HD, 6 + m % 2, 0:P], val[:, k, c:c + HD],
                                         probT[:, n % 2, j * P:(j + 1) * P], start=(j == 0), stop=(j == NG * w - 1))
                last.then_inc(o_ps, 1)

            N = len(units)
            for n in range(N + 2):
                if n < N:
                    scores(n)
                if 1 <= n <= N:
                    turn_probs(n - 1)
                if n >= 2:
                    outputs(n - 2)
            pe.wait_ge(o_ok, H // 2 * TT)
            pe.wait_ge(max_ok, N)
            tok_rows(0, att_o, (0, 1), (atth, attl), True, True)
            after_norm(2)

            pe.wait_ge(wr_in, 16)
            for t in range(TT):
                for k in range(KD):
                    last = pe.matmul(ps[:, 0, t * E:(t + 1) * E], chan[:, k, t * P:(t + 1) * P], wr[:, k, :],
                                     start=(k == 0), stop=(k == KD - 1))
            last.then_inc(log_ps, 1)
            pe.wait_ge(sel_ok, 1)
            pe.matmul(ps[:, 1, 0:E], tri, sel[:, 0:E, 0], start=True, stop=True)
            pe.matmul(ps[:, 1, E:2 * E], tri, sel[:, 0:E, 1], start=True, stop=False)
            pe.matmul(ps[:, 1, E:2 * E], ones[:], sel[:, 0:E, 0], start=False, stop=True)
            pe.matmul(ps[:, 1, 2 * E:3 * E], ones[:], sel[:, 0:E, 0], start=True, stop=False)
            pe.matmul(ps[:, 1, 2 * E:3 * E], ones[:], sel[:, 0:E, 1], start=False, stop=True).then_inc(rank_ps, 1)
            pe.wait_ge(tok_ok, 2 * 3)

            def gather():
                for k in range(KD):
                    for t in range(TT):
                        last = pe.matmul(banks(2, 2)[:, k * P:(k + 1) * P], tok[:, t, k * P:(k + 1) * P],
                                         pick[:, t, :], start=(t == 0), stop=(t == TT - 1))
                last.then_inc(xe_ps, 1)

            def expert(j, rnd):
                def gate_up(c, part):
                    for q in range(2):
                        hi, lo = (as_cols(w) for w in piece(expert_w, AT[("gate", "up")[part], c] + q, j))
                        for k in range(KD):
                            last = product(ps[:, 2 * (c % 2) + part, q * QI:(q + 1) * QI], (xeh[:, k, :], xel[:, k, :]),
                                           (hi[:, k, :], lo[:, k, :]), k == 0, k == KD - 1)
                        last.then_inc(pieces, 1)

                def turn_hid(c):
                    pe.wait_ge(ehid, j * NC + c + 1)
                    for i in range(CT):
                        last = pe.transpose(ps[:, 6, i * P:(i + 1) * P], hid[:, i * P:(i + 1) * P], ident)
                    last.then_inc(ht_ps, 1)

                def down(c):
                    pe.wait_ge(ht_ok, j * NC + c + 1)
                    for q in range(2):
                        hi, lo = (as_rows(w) for w in piece(expert_w, AT["down", c] + q, j))
                        for i in range(2):
                            n = 2 * q + i
                            b = slice(n * P, (n + 1) * P)
                            for h in range(HALF):
                                d = slice(h * BANK, (h + 1) * BANK)
                                last = product(ps[:, 4 + h, :], (hTh[:, c % 2, b], hTl[:, c % 2, b]),
                                               (hi[:, i, d], lo[:, i, d]), c == 0 and n == 0, c == NC - 1 and n == CT - 1)
                        last.then_inc(pieces, 1)

                pe.wait_ge(xe_ok, j + 1 + rnd)
                for c in range(NC):
                    if c == 1:
                        pe.wait_ge(comb_ok, j * 2 + 1)
                    gate_up(c, 0)
                    if c:
                        turn_hid(c - 1)
                    gate_up(c, 1)
                    if 0 < c < NC - 1:
                        down(c - 1)
                    if c == 2:
                        pe.wait_ge(wsel_ok, j + 1)
                        for t in range(TT):
                            last = pe.transpose(ps[:, 7, t * P:(t + 1) * P], wsel[:, t, :], ident)
                        last.then_inc(wT_ps, 1)
                pe.wait_ge(pick_ok, j + 2 + rnd)
                gather()
                turn_hid(NC - 1)
                down(NC - 2)
                down(NC - 1)
                pe.wait_ge(ye_ok, j * 2 + 2)
                pe.wait_ge(wT_ok, j + 1)
                pe.wait_ge(xe_ok, j + 2 + rnd)
                for t in range(TT):
                    for h in range(HALF):
                        last = pe.matmul(ps[:, 2 * t + h, :], back[:, t * P:(t + 1) * P], ye[:, h * BANK:(h + 1) * BANK],
                                         start=True, stop=True)
                    last.then_inc(comb_ps, 1)
                pe.wait_ge(comb_ok, j * 2 + 2)

            pe.wait_ge(pick_ok, 1)
            gather()
            with pe.Fori(0, E) as j:
                expert(j, 0)
            pe.wait_ge(flag_ok, 1)
            over = pe.value_load(flag[0:1, 0:1], min_val=0, max_val=1)
            with pe.If(over > 0):
                pe.wait_ge(pick_ok, E + 2)
                pe.wait_ge(comb_ok, 2 * E + 1)
                gather()
                with pe.Fori(E, 2 * E) as j:
                    expert(j, 1)
            with pe.Else():
                pe.nop()

        @block.scalar
        def _(act):
            G, B = 0, 4 * KD

            def round_piece(phase, k, rnd=0):
                act.wait_ge(landed[phase.raw(k)], phase.landed(k, rnd))
                if not isinstance(rnd, int) or phase.done(k, rnd) >= SPLIT:
                    act.wait_ge(pieces, phase.done(k + 1 - SPLIT, rnd))
                act.copy(wh[:, phase.split(k), :], raw[:, phase.raw(k), :]).then_inc(high_ok, 1)

            def chan_half(n):
                src = banks(4, 2).rearrange("p (k t) -> p k t", t=SEQ)
                act.wait_ge(xT_ps, n + 1)
                if n == 0:
                    act.copy(chan[:, 4:8, :], src).then_inc(chan_a, 1)
                else:
                    for k in range(4, 8):
                        c = (n - 1) * KD + k
                        last = act.activation(chan[:, k, :], src[:, k - 4, :], ACT.Identity, scale=pcol[:, G + c:G + c + 1],
                                              bias=pcol[:, B + c:B + c + 1])
                    last.then_inc(chan_a, 1)
                act.wait_ge(chan_a, n + 1)
                act.copy(chh[:, 4:8, :], chan[:, 4:8, :]).then_inc(ch_high, 1)
                act.wait_ge(chan_d, n + 1)
                act.copy(chh[:, 0:4, :], chan[:, 0:4, :]).then_inc(ch_high, 1)

            def normalise(n):
                for t in range(TT):
                    act.wait_ge(var_ok, TT * n + t + 1)
                    act.activation(mv[:, t, 2:3], mv[:, t, 1:2], ACT.Sqrt).then_inc(dev_ok, 1)
                for t in range(TT):
                    act.wait_ge(res_ok, TT * n + t + 1)
                    act.activation(tok[:, t, :], res[:, t, :], ACT.Identity, scale=mv[:, t, 2:3],
                                   bias=mv[:, t, 3:4]).then_inc(norm_ok, 1)
                if n < 3:
                    chan_half(n + 1)

            chan_half(0)
            for k in range(2):
                round_piece(conv_w, k)
            with act.Fori(0, NCA) as i:
                round_piece(conv_w, 2, i)
                round_piece(conv_w, 3, i)
                act.wait_ge(pieces, conv_w.done(2, i))
                act.wait_ge(mixT_ok, i + 1)
                act.copy(gateB, banks(0, 2).rearrange("p (c t) -> p c t", c=CT)).then_inc(gate_sb, 1)
                round_piece(conv_w, 4, i)
                round_piece(conv_w, 5, i)
                act.wait_ge(pieces, conv_w.done(4, i))
                act.copy(gateC, banks(6, 2).rearrange("p (c t) -> p c t", c=CT)).then_inc(gate_sb, 1)
                round_piece(conv_w, 6, i)
                round_piece(conv_w, 7, i)
            round_piece(conv_o, 2)
            round_piece(conv_o, 3)
            round_piece(dense_0, 0)
            round_piece(dense_0, 1)
            normalise(0)

            def silu_dense(i, width, done):
                act.wait_ge(pieces, done)
                if not isinstance(i, int) or i > 0:
                    act.wait_ge(hid_ok, i)
                act.activation(sgd[:, 0:width], banks(0, 2)[:, 0:width], ACT.Silu).then_inc(silu_ok, 1)

            round_piece(dense_w, 0)
            round_piece(dense_w, 1)
            silu_dense(0, CT * SEQ, dense_0.done(2))
            with act.Fori(0, NFULL - 1) as i:
                for k in (2, 3, 4, 5):
                    round_piece(dense_w, k, i)
                silu_dense(i + 1, CT * SEQ, dense_w.done(4, i))
                for k in (6, 7):
                    round_piece(dense_w, k, i)
            for k in (2, 3, 4):
                round_piece(dense_z, k)
            silu_dense(NFULL, QI // P * SEQ, dense_z.done(3))
            for k in (5, 6, 7, 8):
                round_piece(dense_z, k)
            normalise(1)

            with act.Fori(0, NG) as g:
                round_piece(qkv_w, 2, g)
                round_piece(qkv_w, 3, g)
                act.wait_ge(pieces, qkv_w.done(2, g))
                act.copy(keyT[:, bass.ds(g * CT, CT), :], banks(0, 2).rearrange("p (c t) -> p c t", c=CT)).then_inc(kq_ok, 1)
                round_piece(qkv_w, 4, g)
                round_piece(qkv_w, 5, g)
                act.wait_ge(pieces, qkv_w.done(4, g))
                act.copy(qryT[:, bass.ds(g * CT, CT), :], banks(2, 2).rearrange("p (c t) -> p c t", c=CT)).then_inc(kq_ok, 1)
                round_piece(qkv_w, 6, g)
                round_piece(qkv_w, 7, g)

            def exp_unit(n):
                w = NG * ((n // 2 % 2) + 1) * P
                act.wait_ge(max_ok, n + 1)
                act.activation(masked[:, n % 2, 0:w], masked[:, n % 2, 0:w], ACT.Exp, scale=SCALE,
                               bias=soft[:, n % 2, 1:2], accum_out=soft[:, n % 2, 2:3]).then_inc(exp_ok, 1)

            def copy_probs(n):
                w = NG * ((n // 2 % 2) + 1) * P
                act.wait_ge(pT_ps, n + 1)
                if n >= 2:
                    act.wait_ge(o_ps, n - 1)
                act.copy(probT[:, n % 2, 0:w], banks(4, 2)[:, 0:w]).then_inc(pT_ok, 1)

            for n in range(TT * H + 1):
                if n < TT * H:
                    exp_unit(n)
                if n >= 1:
                    copy_probs(n - 1)
            normalise(2)

            act.wait_ge(lgap_ok, 1)
            act.activation(gate2[:, 1, :], gate2[:, 0, :], ACT.Exp).then_inc(lexp_ok, 1)

            def round_xe(n):
                act.wait_ge(xe_ps, n)
                act.copy(xeh, banks(2, 2).rearrange("p (k s) -> p k s", k=KD)).then_inc(xe_high, 1)

            def expert(j, rnd):
                for n in range(PER_EXPERT):
                    part, c = ORDER[n // 2]
                    if n == AT["gate", 1]:
                        silu(j, 0)
                    if part == "down" and c < NC - 1 and n % 2 == 0:
                        silu(j, c + 1)
                        round_hid(j, c)
                    if n == AT["down", 2]:
                        act.wait_ge(wT_ps, j + 1)
                        act.copy(back, ps[:, 7, 0:SEQ]).then_inc(wT_ok, 1)
                    if n == AT["down", NC - 1] + 1:
                        round_xe(j + 2 + rnd)
                        round_hid(j, NC - 1)
                    round_piece(expert_w, n, j)
                act.wait_ge(pieces, expert_w.done(PER_EXPERT, j))
                act.copy(ye[:, 0:BANK], ps[:, 4, :]).then_inc(ye_ok, 1)

            def silu(j, c):
                act.wait_ge(pieces, expert_w.done(AT["gate", c] + 2, j))
                act.activation(sg[:, c % 2, :], ps[:, 2 * (c % 2), :], ACT.Silu).then_inc(esilu, 1)

            def round_hid(j, c):
                act.wait_ge(ht_ps, j * NC + c + 1)
                act.copy(hTh[:, c % 2, :], ps[:, 6, :]).then_inc(ht_high, 1)

            round_xe(1)
            with act.Fori(0, E) as j:
                expert(j, 0)
            act.wait_ge(flag_ok, 1)
            over = act.value_load(flag[0:1, 0:1], min_val=0, max_val=1)
            with act.If(over > 0):
                round_xe(E + 2)
                with act.Fori(E, 2 * E) as j:
                    expert(j, 1)
            with act.Else():
                act.nop()
            normalise(3)

        @block.vector
        def _(dve):
            chain = Chain(dve, dve_steps)
            G, B, C = 0, 4 * KD, 8 * KD

            def rest_piece(phase, k, rnd=0):
                dve.wait_ge(high_ok, phase.done(k + 1, rnd))
                s = phase.split(k)
                dve.tensor_tensor(wl[:, s, :], raw[:, phase.raw(k), :], wh[:, s, :].bitcast(F32),
                                  ALU.subtract).then_inc(low_ok, 1)

            def chan_half(n):
                dve.wait_ge(xT_ps, n + 1)
                src = banks(2, 2).rearrange("p (k t) -> p k t", t=SEQ)
                if n == 0:
                    dve.tensor_copy(chan[:, 0:4, :], src).then_inc(chan_d, 1)
                else:
                    for k in range(4):
                        c = (n - 1) * KD + k
                        last = dve.tensor_scalar(chan[:, k, :], src[:, k, :], pcol[:, G + c:G + c + 1],
                                                 pcol[:, B + c:B + c + 1], ALU.mult, ALU.add)
                    last.then_inc(chan_d, 1)
                for m, half in enumerate((slice(4, 8), slice(0, 4))):
                    dve.wait_ge(ch_high, 2 * n + m + 1)
                    if m:
                        dve.wait_ge(chan_d, n + 1)
                    dve.tensor_tensor(chl[:, half, :], chan[:, half, :], chh[:, half, :].bitcast(F32),
                                      ALU.subtract).then_inc(ch_low, 1)

            def statistics(t):
                for h in range(HALF):
                    last = dve.bn_stats(stats[:, t, h, :], res[:, t, h * BANK:(h + 1) * BANK])
                chain.link(last)
                chain.link(dve.bn_aggr(mv[:, t, 0:2], stats[:, t, :, :]))
                dve.tensor_scalar(mv[:, t, 1:2], mv[:, t, 1:2], EPS, None, ALU.add).then_inc(var_ok, 1)

            def scales(n, t):
                dve.wait_ge(dev_ok, TT * n + t + 1)
                chain.link(dve.reciprocal(mv[:, t, 2:3], mv[:, t, 2:3]))
                dve.tensor_scalar(mv[:, t, 3:4], mv[:, t, 0:1], mv[:, t, 2:3], -1.0, ALU.mult, ALU.mult).then_inc(res_ok, 1)

            def residual(n, bank, done):
                dve.wait_ge(pieces, done)
                if n:
                    dve.wait_ge(tok_ok, 2 * n)
                for t in range(TT):
                    chain.link(dve.scalar_tensor_tensor(out=res[:, t, :], in0=tok[:, t, :], scalar=ALPHA,
                                                        in1=banks(bank + 2 * t, 2), op0=ALU.mult, op1=ALU.add))
                    statistics(t)
                for t in range(TT):
                    scales(n, t)
                chan_half(n + 1)

            dve.memset(upad[:, :, 0:CW - 1], 0.0).then_inc(mixT_ok, 1)
            dve.wait_ge(par_t, 1)
            dve.tensor_copy(pcol[:], ps[:, 0, 0:P]).then_inc(par_done, 1)
            chan_half(0)
            dve.memset(soft[:], 0.0).then_inc(v_ok, 1)
            for k in range(2):
                rest_piece(conv_w, k)

            def taps(w, i, c):
                return pcol[:, bass.ds(i * CT + (C + w * KD + c), 1)]

            with dve.Fori(0, NCA) as i:
                for k in range(2, 8):
                    rest_piece(conv_w, k, i)
                dve.wait_ge(pieces, conv_w.done(6, i))
                dve.wait_ge(gate_sb, i * 2 + 2)
                dve.tensor_tensor(upad[:, :, CW - 1:], banks(2, 2).rearrange("p (c t) -> p c t", c=CT), gateC,
                                  ALU.mult).then_inc(u_read, 1)
                dve.wait_ge(u_read, i + 1)
                for c in range(CT):
                    last = dve.tensor_scalar(conv[:, c, :], upad[:, c, 0:SEQ], taps(0, i, c), None, ALU.mult)
                last.then_inc(conv_ok, 1)
                for w in range(1, CW):
                    dve.wait_ge(conv_ok, i * CW + w)
                    for c in range(CT):
                        last = dve.scalar_tensor_tensor(out=conv[:, c, :], in0=upad[:, c, w:w + SEQ], scalar=taps(w, i, c),
                                                        in1=conv[:, c, :], op0=ALU.mult, op1=ALU.add)
                    last.then_inc(conv_ok, 1)
                dve.wait_ge(conv_ok, i * CW + CW)
                dve.tensor_tensor(conv, conv, gateB, ALU.mult).then_inc(msplit, 1)
                dve.wait_ge(msplit, i * 2 + 1)
                dve.tensor_copy(mixh[:, bass.ds(i * CT, CT), :], conv).then_inc(msplit, 1)
                dve.wait_ge(msplit, i * 2 + 2)
                dve.tensor_tensor(mixl[:, bass.ds(i * CT, CT), :], conv, mixh[:, bass.ds(i * CT, CT), :].bitcast(F32),
                                  ALU.subtract).then_inc(mixT_ok, 1)
            rest_piece(conv_o, 2)
            rest_piece(conv_o, 3)
            rest_piece(dense_0, 0)
            rest_piece(dense_0, 1)
            residual(0, 4, conv_o.done(4))

            def hidden(i, w, done):
                dve.wait_ge(silu_ok, i + 1)
                dve.wait_ge(pieces, done)
                flat = [a.rearrange("p c t -> p (c t)")[:, 0:w] for a in (hidh, hidl)]
                dve.tensor_tensor(sgd[:, 0:w], banks(2, 2)[:, 0:w], sgd[:, 0:w], ALU.mult).then_inc(hsplit, 1)
                dve.wait_ge(hsplit, i * 2 + 1)
                dve.tensor_copy(flat[0], sgd[:, 0:w]).then_inc(hsplit, 1)
                dve.wait_ge(hsplit, i * 2 + 2)
                dve.tensor_tensor(flat[1], sgd[:, 0:w], flat[0].bitcast(F32), ALU.subtract).then_inc(hid_ok, 1)

            rest_piece(dense_w, 0)
            rest_piece(dense_w, 1)
            with dve.Fori(0, NFULL - 1) as i:
                rest_piece(dense_w, 2, i)
                rest_piece(dense_w, 3, i)
                hidden(i, CT * SEQ, dense_w.done(2, i))
                for k in range(4, 8):
                    rest_piece(dense_w, k, i)
            rest_piece(dense_z, 2)
            rest_piece(dense_z, 3)
            hidden(NFULL - 1, CT * SEQ, dense_z.done(2))
            for k in range(4, 8):
                rest_piece(dense_z, k)
            hidden(NFULL, QI // P * SEQ, dense_z.done(6))
            rest_piece(dense_z, 8)
            residual(1, 4, dense_z.done(7))

            with dve.Fori(0, NG) as g:
                for k in range(2, 8):
                    rest_piece(qkv_w, k, g)
                dve.wait_ge(pieces, qkv_w.done(6, g))
                dve.tensor_copy(val[:, :, bass.ds(g * AW, AW)], ps[:, 4:4 + TT, :]).then_inc(v_ok, 1)

            def maximum(n):
                t = n // 2 % 2
                w = (t + 1) * P
                dve.wait_ge(sc_ps, n + 1)
                if n >= 2:
                    dve.wait_ge(pT_ps, n - 1)
                src = banks(2 * (n % 2), 2)[:, 0:NG * SEQ].rearrange("p (g k) -> p g k", g=NG)[:, :, 0:w]
                m = (masks if t else masks[:, :, 1:2, :]).rearrange("p g k s -> p g (k s)") if t else masks[:, :, 1, :]
                dst = masked[:, n % 2, 0:NG * w].rearrange("p (g k) -> p g k", g=NG)
                chain.link(dve.tensor_tensor_reduce(out=dst, in0=src, in1=m, scale=1.0, scalar=-3.0e38,
                                                    op0=ALU.add, op1=ALU.max, accum_out=soft[:, n % 2, 0:1]))
                dve.tensor_scalar(soft[:, n % 2, 1:2], soft[:, n % 2, 0:1], -SCALE, None, ALU.mult).then_inc(max_ok, 1)

            def divide(n):
                w = NG * ((n // 2 % 2) + 1) * P
                dve.wait_ge(exp_ok, n + 1)
                chain.link(dve.reciprocal(soft[:, n % 2, 3:4], soft[:, n % 2, 2:3]))
                dve.tensor_scalar(masked[:, n % 2, 0:w], masked[:, n % 2, 0:w], soft[:, n % 2, 3:4], None,
                                  ALU.mult).then_inc(prob_ok, 1)

            def keep_outputs(m):
                dve.wait_ge(o_ps, 2 * m + 2)
                t = m % TT
                c = slice(t * P, (t + 1) * P)
                src = ps[:, 6 + m % 2, 0:P]
                chain.link(dve.tensor_copy(atth[:, m // TT, c], src))
                dve.tensor_tensor(attl[:, m // TT, c], src, atth[:, m // TT, c].bitcast(F32), ALU.subtract).then_inc(o_ok, 1)

            N = H * TT
            for n in range(N + 3):
                if n < N:
                    maximum(n)
                if 1 <= n <= N:
                    divide(n - 1)
                if n >= 3 and (n - 3) % 2 == 1:
                    keep_outputs((n - 3) // 2)
            residual(2, 0, att_o.done(2))

            dve.wait_ge(log_ps, 1)
            dve.tensor_copy(lg[:], ps[:, 0, 0:TT * E].rearrange("p (t e) -> p t e", t=TT))
            chain.link(dve.tensor_scalar(prio[:], slots[:, 0:E], -1.0, float(P), ALU.mult, ALU.add))
            for choice in range(2):
                chain.link(dve.tensor_reduce(top[:, choice, :], lg[:], AX_X, ALU.max))
                for t in range(TT):
                    last = dve.scalar_tensor_tensor(out=pr[:, t, :], in0=lg[:, t, :], scalar=top[:, choice, t:t + 1],
                                                    in1=prio[:], op0=ALU.is_equal, op1=ALU.mult)
                chain.link(last)
                chain.link(dve.tensor_reduce(pm[:], pr[:], AX_X, ALU.max))
                for t in range(TT):
                    last = dve.tensor_scalar(hot[:, choice, t, :], pr[:, t, :], pm[:, t:t + 1], None, ALU.is_equal)
                chain.link(last)
                if choice == 0:
                    chain.link(dve.scalar_tensor_tensor(out=lg[:], in0=hot[:, 0, :, :], scalar=-3.0e38, in1=lg[:],
                                                        op0=ALU.mult, op1=ALU.add))
            dve.tensor_tensor(gate2[:, 0, :], top[:, 1, :], top[:, 0, :], ALU.subtract).then_inc(lgap_ok, 1)
            dve.memset(sel[:, E:E + 1, :], 0.0)
            dve.memset(rank[:, E:E + 1, :], 0.0)
            dve.tensor_tensor(sel[:, 0:E, :], hot[:, 0, :, :].rearrange("p t e -> p e t"),
                              hot[:, 1, :, :].rearrange("p t e -> p e t"), ALU.add).then_inc(sel_ok, 1)
            dve.wait_ge(lexp_ok, 1)
            chain.link(dve.tensor_scalar(gate2[:, 3, :], gate2[:, 1, :], 1.0, None, ALU.add))
            chain.link(dve.reciprocal(gate2[:, 2, :], gate2[:, 3, :]))
            chain.link(dve.tensor_tensor(gate2[:, 3, :], gate2[:, 1, :], gate2[:, 2, :], ALU.mult))
            for t in range(TT):
                last = dve.tensor_scalar(comb[:, 0:E, t], hot[:, 0, t, :], gate2[:, 2, t:t + 1], None, ALU.mult)
            chain.link(last)
            for t in range(TT):
                dve.scalar_tensor_tensor(out=comb[:, 0:E, t], in0=hot[:, 1, t, :], scalar=gate2[:, 3, t:t + 1],
                                         in1=comb[:, 0:E, t], op0=ALU.mult, op1=ALU.add)
            dve.wait_ge(rank_ps, 1)
            chain.link(dve.tensor_copy(rank[:, 0:E, :], ps[:, 1, 0:TT * E].rearrange("p (t e) -> p e t", t=TT)))

            def picker(dst, e, values, done):
                for t in range(TT):
                    last = dve.tensor_scalar(dst[:, t, :], slots, rank[:, bass.ds(e, 1), t], values[:, bass.ds(e, 1), t],
                                             ALU.is_equal, ALU.mult)
                last.then_inc(done, 1)

            picker(pick, 0, sel, pick_ok)
            chain.link(dve.tensor_reduce(peak[:], ps[:, 1, 2 * E:3 * E], AX_X, ALU.max))
            chain.link(dve.tensor_scalar(flag[:], peak[:], float(P), None, ALU.is_gt))
            dve.wait_ge(tok_ok, 2 * 3)
            dve.tensor_scalar(res[:], tok[:], ALPHA, None, ALU.mult).then_inc(comb_ok, 1)
            dve.engine_nop().then_inc(flag_ok, 1)

            def rest_xe(n):
                dve.wait_ge(xe_high, n)
                dve.tensor_tensor(xel, banks(2, 2).rearrange("p (k s) -> p k s", k=KD), xeh.bitcast(F32),
                                  ALU.subtract).then_inc(xe_ok, 1)

            def expert(j, e, rnd):
                def rest_hid(c):
                    dve.wait_ge(ht_high, j * NC + c + 1)
                    dve.tensor_tensor(hTl[:, c % 2, :], ps[:, 6, :], hTh[:, c % 2, :].bitcast(F32),
                                      ALU.subtract).then_inc(ht_ok, 1)

                def hidden(c):
                    dve.wait_ge(esilu, j * NC + c + 1)
                    dve.wait_ge(pieces, expert_w.done(AT["up", c] + 2, j))
                    dve.tensor_tensor(hid, ps[:, 2 * (c % 2) + 1, :], sg[:, c % 2, :], ALU.mult).then_inc(ehid, 1)

                for n in range(PER_EXPERT):
                    part, c = ORDER[n // 2]
                    if n == 3:
                        picker(wsel, e, comb, wsel_ok)
                        picker(pick, e + 1, sel, pick_ok)
                    if n % 2 == 0 and part == "down" and c < NC - 1:
                        rest_hid(c)
                    for h in range(NC):
                        if n == AT["up", h] + 4:
                            hidden(h)
                    if n == AT["down", NC - 1] + 1:
                        rest_xe(j + 2 + rnd)
                        rest_hid(NC - 1)
                    rest_piece(expert_w, n, j)
                dve.wait_ge(pieces, expert_w.done(PER_EXPERT, j))
                dve.tensor_copy(ye[:, BANK:D], ps[:, 5, :]).then_inc(ye_ok, 1)
                for t in range(TT):
                    dve.wait_ge(comb_ps, j * 2 + t + 1)
                    dve.tensor_tensor(res[:, t, :], banks(2 * t, 2), res[:, t, :], ALU.add).then_inc(comb_ok, 1)
                dve.wait_ge(comb_ok, j * 2 + 3)

            rest_xe(1)
            with dve.Fori(0, E) as j:
                expert(j, j, 0)
            over = dve.value_load(flag[0:1, 0:1], min_val=0, max_val=1)
            with dve.If(over > 0):
                dve.tensor_scalar(rank[:], rank[:], -float(P), None, ALU.add).then_inc(rank_ok, 1)
                dve.wait_ge(rank_ok, 1)
                picker(pick, 0, sel, pick_ok)
                rest_xe(E + 2)
                with dve.Fori(E, 2 * E) as j:
                    expert(j, j - E, 1)
            with dve.Else():
                dve.nop()
            for t in range(TT):
                statistics(t)
            for t in range(TT):
                scales(3, t)
            dve.wait_ge(gb_in, 32 * 4)
            for t in range(TT):
                dve.wait_ge(norm_ok, TT * 3 + t + 1)
                chain.link(dve.tensor_tensor(res[:, t, :], tok[:, t, :], gb[:, 0, :], ALU.mult))
                dve.tensor_tensor(res[:, t, :], res[:, t, :], gb[:, 1, :], ALU.add).then_inc(fin_ok, 1)


def launch_tables(P, window_spans):
    import numpy as np

    q = np.arange(P)[:, None]
    k = np.arange(P)[None, :]
    out = []
    for span, dil in window_spans:
        for back in (P, 0):
            dist = back + q - k
            ok = (dist >= 0) & (dist % dil == 0) & (dist <= span * dil)
            out.append(np.where(ok, 0.0, FAR))
    out.append(np.eye(P))
    out.append(q < k)
    out.append(np.broadcast_to(k, (P, P)))
    return np.stack([np.asarray(a, np.float32) for a in out])


_INS = ['x', 'a_w_in', 'a_conv', 'a_w_out', 'kv_w', 'b_w_q', 'b_w_o', 'ffn_w_gate', 'ffn_w_up', 'ffn_w_down',
        'moe_w_router', 'moe_w_gate', 'moe_w_up', 'moe_w_down', 'ln_g', 'ln_b']


def kernel(**inputs):
    import numpy as _np
    import concourse.bacc as _bacc
    from concourse import mybir as _mybir
    from concourse.bass_utils import run_bass_kernel_spmd as _run

    nc = _bacc.Bacc("TRN2", target_bir_lowering=False, num_devices=1)
    arrays, args = {}, []
    for name in _INS:
        a = _np.ascontiguousarray(inputs[name])
        arrays[f"in_{name}_dram"] = a
        args.append(nc.dram_tensor(f"in_{name}_dram", a.shape, _mybir.dt.from_np(a.dtype), kind="ExternalInput").ap())
    tables = launch_tables(128, ((128, 1), (128, 4), (128, 16)))
    arrays["tables_dram"] = tables
    args.append(nc.dram_tensor("tables_dram", tables.shape, _mybir.dt.float32, kind="ExternalInput").ap())
    args.append(nc.dram_tensor("out_0_dram", inputs["x"].shape, _mybir.dt.float32, kind="ExternalOutput").ap())
    hybrid_trunk(nc, *args)
    r = _run(nc, [arrays], core_ids=[0])
    return r.results[0]["out_0_dram"]
```

```python
from contextlib import ExitStack

import concourse.bass as bass
from concourse import mybir

F32 = mybir.dt.float32
F32R = mybir.dt.float32r
I32 = mybir.dt.int32
BF16 = mybir.dt.bfloat16
ALU = mybir.AluOpType
ACT = mybir.ActivationFunctionType
AX_X = mybir.AxisListType.X

P = 128
BANK = 512
ITEM = 2048
RAW = 6
SPLIT = 3
FAR = -1.0e30


class Chain:

    def __init__(self, eng, sem):
        self.eng, self.sem, self.n = eng, sem, 0

    def link(self, ins):
        ins.then_inc(self.sem, 1)
        self.n += 1
        self.eng.wait_ge(self.sem, self.n)


def hybrid_trunk(nc, x, a_w_in, a_conv, a_w_out, kv_w, b_w_q, b_w_o, ffn_w_gate, ffn_w_up, ffn_w_down,
                 moe_w_router, moe_w_gate, moe_w_up, moe_w_down, ln_g, ln_b, tables, out):
    _, SEQ, D = x.shape
    DEPTH = ln_g.shape[0]
    ALPHA = (2.0 * DEPTH) ** 0.25
    EPS = 1e-5
    F = ffn_w_gate.shape[2]
    E = moe_w_gate.shape[1]
    FE = moe_w_gate.shape[3]
    CW = a_conv.shape[1]
    AW = b_w_o.shape[1]
    HD = 64
    H = AW // HD
    NG = b_w_q.shape[2] // AW
    TT = SEQ // P
    KD = D // P
    HALF = D // BANK
    CH = 512
    CT = CH // P
    QI = 256
    assert TT == 2 and KD == 8 and HALF == 2 and CW == 3 and H == 8 and NG == 3 and E == 8
    assert KD * QI == ITEM and 2 * D == ITEM
    NCA = D // CH
    NFULL = F // CH
    assert F - NFULL * CH == QI
    NC = FE // CH
    assert NC * CH == FE and NC % 2 == 1
    PER_EXPERT = 6 * NC
    assert PER_EXPERT % (RAW + 1) == 0 and PER_EXPERT % SPLIT == 0 and RAW % SPLIT == 0
    SCALE = HD ** -0.5
    WARM_X, WARM_W, WARM_NORM, WARM_CHAN, WARM_ROUTER, WARM_XE = 10, 10, 14, 14, 5, 10

    with ExitStack() as ctx:
        def sb(name, shape, dt=F32):
            return ctx.enter_context(nc.sbuf_tensor(name, shape, dt))

        def sem(name):
            return ctx.enter_context(nc.semaphore(name))

        raw = sb("raw", [P, RAW, ITEM])
        wh = sb("wh", [P, SPLIT, ITEM], F32R)
        wl = sb("wl", [P, SPLIT, ITEM], F32R)
        tok = sb("tok", [P, TT, D])
        chh = sb("chh", [P, KD, SEQ], F32R)
        chl = sb("chl", [P, KD, SEQ], F32R)
        parts = sb("parts", [P, 2, ITEM], F32R)
        res = sb("res", [P, TT, D])
        gb = sb("gb", [P, 2, D])
        tab = sb("tab", [P, 9, P])
        NPAR = (8 + CW) * KD
        pcol = sb("pcol", [P, NPAR])
        zero = sb("zero", [P, BANK], BF16)
        ones = sb("ones", [P, P])
        wr = sb("wr", [P, KD, E])
        flag = sb("flag", [P, 1], I32)
        stats = sb("stats", [P, TT, HALF, 6])
        mv = sb("mv", [P, TT, 4])
        soft = sb("soft", [P, 2, 4])
        lg = sb("lg", [P, TT, E])
        pr = sb("pr", [P, TT, E])
        prio = sb("prio", [P, E])
        hot = sb("hot", [P, 2, TT, E])
        top = sb("top", [P, 2, TT])
        pm = sb("pm", [P, TT])
        gate2 = sb("gate2", [P, 4, TT])
        sel = sb("sel", [P, E, TT])
        comb = sb("comb", [P, E, TT])
        rank = sb("rank", [P, E, TT])
        peak = sb("peak", [P, 1])
        arena = sb("arena", [P, 12288])

        cut = [0]

        def view(size, fresh=False):
            if fresh:
                cut[0] = 0
            a = arena[:, cut[0]:cut[0] + size]
            cut[0] += size
            assert cut[0] <= 12288
            return a

        prow = arena[:, 12288 - P:]
        UPAD = SEQ + CW - 1
        gateB = view(CT * SEQ, True).rearrange("p (c t) -> p c t", c=CT)
        gateC = view(CT * SEQ).rearrange("p (c t) -> p c t", c=CT)
        upad = view(CT * UPAD).rearrange("p (c t) -> p c t", c=CT)
        conv = view(CT * SEQ).rearrange("p (c t) -> p c t", c=CT)
        mixh = parts[:, 0, :].rearrange("p (c t) -> p c t", c=KD)
        mixl = parts[:, 1, :].rearrange("p (c t) -> p c t", c=KD)
        chan = view(KD * SEQ, True).rearrange("p (c t) -> p c t", c=KD)
        sgd = view(CT * SEQ)
        hidh = parts[:, 0, :].rearrange("p (c t) -> p c t", t=SEQ)
        hidl = parts[:, 1, :].rearrange("p (c t) -> p c t", t=SEQ)
        NQ = NG * AW // P
        keyT = view(NQ * SEQ, True).rearrange("p (c t) -> p c t", c=NQ)
        qryT = view(NQ * SEQ).rearrange("p (c t) -> p c t", c=NQ)
        val = view(TT * NG * AW).rearrange("p (t n) -> p t n", t=TT)
        mask2 = view(2 * NG * SEQ).rearrange("p (b n) -> p b n", b=2)
        masked = [mask2[:, 0, :], mask2[:, 1, :], res[:, 0, 0:NG * SEQ], res[:, 1, 0:NG * SEQ]]
        probT = view(2 * NG * SEQ).rearrange("p (b n) -> p b n", b=2)
        atth = parts[:, 0, 0:H // 2 * SEQ].rearrange("p (c t) -> p c t", c=H // 2)
        attl = parts[:, 1, 0:H // 2 * SEQ].rearrange("p (c t) -> p c t", c=H // 2)
        view(KD * SEQ, True)
        pick = view(SEQ).rearrange("p (t s) -> p t s", t=TT)
        back = view(SEQ)
        sg = view(2 * CH).rearrange("p (b n) -> p b n", b=2)
        hid = view(CH)
        ye = view(D)
        wsel = view(SEQ).rearrange("p (t s) -> p t s", t=TT)
        raw_more = view(ITEM)
        xeh = parts[:, 0, 0:KD * P].rearrange("p (k s) -> p k s", k=KD)
        xel = parts[:, 1, 0:KD * P].rearrange("p (k s) -> p k s", k=KD)
        hTh = parts[:, 0, KD * P:KD * P + 2 * CH].rearrange("p (b n) -> p b n", b=2)
        hTl = parts[:, 1, KD * P:KD * P + 2 * CH].rearrange("p (b n) -> p b n", b=2)

        masks = tab[:, 0:6, :].rearrange("p (g k) s -> p g k s", k=2)
        ident = tab[:, 6, :]
        tri = tab[:, 7, :]
        slots = tab[:, 8, :]

        ps = ctx.enter_context(nc.psum_tensor("ps", [P, 8, BANK], F32))

        def banks(a, n):
            return ps[:, a:a + n, :].rearrange("p b n -> p (b n)")

        landed = [sem(f"landed{i}") for i in range(RAW + 1)]
        high_ok = sem("high_ok")
        low_ok = sem("low_ok")
        pieces = sem("pieces")
        tab_in, par_in, mask_in, gb_in, wr_in = (sem(n) for n in ("tab_in", "par_in", "mask_in", "gb_in", "wr_in"))
        x_in = [sem(f"x_in{t}") for t in range(TT)]
        const_set = sem("const_set")
        dve_steps = sem("dve_steps")
        par_t, par_done = sem("par_t"), sem("par_done")
        conv_ok = sem("conv_ok")
        rank_ok = sem("rank_ok")
        xT_ps = sem("xT_ps")
        chan_a, chan_d = sem("chan_act"), sem("chan_dve")
        ch_high, ch_low = sem("ch_high"), sem("ch_low")
        gate_sb = sem("gate_sb")
        u_read = sem("u_read")
        mixT_ok = sem("mixT_ok")
        res_ok = sem("res_ok")
        var_ok, dev_ok = sem("var_ok"), sem("dev_ok")
        mix_part = sem("mix_part")
        norm_ok = sem("norm_ok")
        tok_ok = sem("tok_ok")
        silu_ok, hid_ok = sem("silu_ok"), sem("hid_ok")
        kq_ok, v_ok = sem("kq_ok"), sem("v_ok")
        sc_ps = sem("sc_ps")
        max_ok = sem("max_ok")
        exp_ok = sem("exp_ok")
        prob_ok = sem("prob_ok")
        pT_ps, pT_ok = sem("pT_ps"), sem("pT_ok")
        o_ps, o_ok = sem("o_ps"), sem("o_ok")
        log_ps, rank_ps = sem("log_ps"), sem("rank_ps")
        lgap_ok, lexp_ok = sem("lgap_ok"), sem("lexp_ok")
        sel_ok = sem("sel_ok")
        flag_ok = sem("flag_ok")
        pick_ok = sem("pick_ok")
        wsel_ok = sem("wsel_ok")
        wT_ps, wT_ok = sem("wT_ps"), sem("wT_ok")
        xe_ps, xe_high, xe_ok = sem("xe_ps"), sem("xe_high"), sem("xe_ok")
        esilu, ehid = sem("esilu"), sem("ehid")
        ht_ps, ht_high, ht_ok = sem("ht_ps"), sem("ht_high"), sem("ht_ok")
        hsplit = sem("hsplit")
        msplit = sem("msplit")
        ye_ok = sem("ye_ok")
        comb_ps, comb_ok = sem("comb_ps"), sem("comb_ok")
        fin_ok, stored = sem("fin_ok"), sem("stored")
        block = ctx.enter_context(nc.Block())

        x_d = x[0].rearrange("(t p) d -> p t d", p=P)
        out_d = out[0].rearrange("(t p) d -> p t d", p=P)

        def cols(w, c0):
            return w.rearrange("(k p) n -> p k n", p=P)[:, :, bass.ds(c0, QI)]

        def rows(w, r0):
            return w[bass.ds(r0, 2 * P), :].rearrange("(i p) d -> p i d", p=P)

        def as_cols(a):
            return a.rearrange("p (k n) -> p k n", k=KD)

        def as_rows(a):
            return a.rearrange("p (i n) -> p i n", i=2)

        total = [0]

        class Phase:
            def __init__(self, per, rounds=1, ring=RAW):
                self.start, self.per, self.ring = total[0], per, ring
                assert rounds == 1 or per % ring == 0
                total[0] += per * rounds

            def done(self, k, rnd=0):
                return rnd * self.per + (self.start + k)

            def landed(self, k, rnd=0):
                if self.ring == RAW:
                    return rnd * (16 * (self.per // RAW)) + 16 * ((self.start + k) // RAW + 1)
                s = self.slot(k)
                before = (self.start - s + RAW - 1) // RAW if s < RAW else 0
                return rnd * (16 * (self.per // self.ring)) + 16 * (before + k // self.ring + 1)

            def slot(self, k):
                if self.ring == RAW:
                    return (self.start + k) % RAW
                n = k % self.ring
                return (self.start + n) % RAW if n < RAW else RAW

            def raw(self, k):
                return raw[:, self.slot(k), :] if self.slot(k) < RAW else raw_more

            def split(self, k):
                return (self.start + k) % SPLIT

        conv_w = Phase(6, NCA)
        conv_o = Phase(4)
        dense_0 = Phase(2)
        dense_w = Phase(6, NFULL - 1)
        dense_z = Phase(7)
        qkv_w = Phase(6, NG)
        att_o = Phase(2)
        ORDER = [("gate", 0), ("up", 0)]
        for c in range(1, NC):
            ORDER += [("gate", c), ("up", c), ("down", c - 1)]
        ORDER += [("down", NC - 1)]
        expert_w = Phase(PER_EXPERT, 2 * E, RAW + 1)
        AT = {what: 2 * n for n, what in enumerate(ORDER)}

        @block.sync
        def _(sp):
            def load(phase, k, view_, src, rnd=0):
                first = isinstance(rnd, int) and rnd == 0 and k < phase.ring
                if first and phase.slot(k) == RAW:
                    sp.wait_ge(mix_part, 2 * (HALF * TT - 1) + 1)
                elif not isinstance(rnd, int) or phase.done(k, rnd) >= RAW:
                    sp.wait_ge(low_ok, phase.done(k + 1 - (RAW if first else phase.ring), rnd))
                sp.dma_start(view_(phase.raw(k)), src).then_inc(landed[phase.slot(k)], 16)

            sp.dma_start(tab[:, 6:9, :], tables[6:9].rearrange("n p s -> p n s")).then_inc(tab_in, 16)
            for t in range(TT):
                sp.dma_start(tok[:, t, :], x_d[:, t, :]).then_inc(x_in[t], 16)
            sp.dma_start(prow[0:4 * KD, :], ln_g.rearrange("l n (k p) -> (l n k) p", p=P)).then_inc(par_in, 16)
            sp.dma_start(prow[4 * KD:8 * KD, :], ln_b.rearrange("l n (k p) -> (l n k) p", p=P)).then_inc(par_in, 16)
            sp.dma_start(prow[8 * KD:(8 + CW) * KD, :], a_conv[0].rearrange("w (k p) -> (w k) p", p=P)).then_inc(par_in, 16)
            for i in range(NCA):
                for part in range(3):
                    for q in range(2):
                        load(conv_w, 2 * part + q, as_cols, cols(a_w_in[0], part * D + i * CH + q * QI), i)
            for q in range(4):
                load(conv_o, q, as_rows, rows(a_w_out[0], q * 2 * P))
            for q in range(2):
                load(dense_0, q, as_cols, cols(ffn_w_gate[0], q * QI))
            with sp.Fori(0, NFULL - 1) as i:
                for q in range(2):
                    load(dense_w, q, as_cols, cols(ffn_w_up[0], i * CH + q * QI), i)
                for q in range(2):
                    load(dense_w, 2 + q, as_cols, cols(ffn_w_gate[0], i * CH + (CH + q * QI)), i)
                for q in range(2):
                    load(dense_w, 4 + q, as_rows, rows(ffn_w_down[0], i * CH + q * 2 * P), i)
            i = NFULL - 1
            for q in range(2):
                load(dense_z, q, as_cols, cols(ffn_w_up[0], i * CH + q * QI))
            load(dense_z, 2, as_cols, cols(ffn_w_gate[0], NFULL * CH))
            load(dense_z, 3, as_cols, cols(ffn_w_up[0], NFULL * CH))
            for q in range(2):
                load(dense_z, 4 + q, as_rows, rows(ffn_w_down[0], i * CH + q * 2 * P))
            load(dense_z, 6, as_rows, rows(ffn_w_down[0], NFULL * CH))
            with sp.Fori(0, NG) as g:
                for q in range(2):
                    load(qkv_w, q, as_cols, cols(kv_w, g * (2 * AW) + q * QI), g)
                for q in range(2):
                    load(qkv_w, 2 + q, as_cols, cols(b_w_q[0], g * AW + q * QI), g)
                for q in range(2):
                    load(qkv_w, 4 + q, as_cols, cols(kv_w, g * (2 * AW) + (AW + q * QI)), g)
            for q in range(2):
                load(att_o, q, as_rows, rows(b_w_o[0], q * 2 * P))

            def expert(j, e):
                wg, wu, wd = (w[0][bass.ds(e, 1)].rearrange("o a b -> (o a) b") for w in (moe_w_gate, moe_w_up, moe_w_down))
                for n, (part, c) in enumerate(ORDER):
                    for q in range(2):
                        if part == "down":
                            load(expert_w, 2 * n + q, as_rows, rows(wd, c * CH + q * 2 * P), j)
                        else:
                            load(expert_w, 2 * n + q, as_cols, cols(wg if part == "gate" else wu, c * CH + q * QI), j)

            expert(0, 0)
            with sp.Fori(1, E) as j:
                expert(j, j)
            sp.wait_ge(flag_ok, 1)
            over = sp.value_load(flag[0:1, 0:1], min_val=0, max_val=1)
            with sp.If(over > 0):
                with sp.Fori(E, 2 * E) as j:
                    expert(j, j - E)
            with sp.Else():
                sp.nop()
            for t in range(TT):
                for h in range(HALF):
                    d = slice(h * BANK, (h + 1) * BANK)
                    sp.wait_ge(fin_ok, HALF * t + h + 1)
                    sp.dma_start(out_d[:, t, d], res[:, t, d]).then_inc(stored, 16)
            sp.wait_ge(stored, 16 * TT * HALF)

        @block.gpsimd
        def _(pool):
            pool.memset(zero[:], 0.0).then_inc(const_set, 1)
            pool.memset(ones[:], 1.0).then_inc(const_set, 1)
            pool.wait_ge(pieces, conv_w.done(2))
            pool.dma_start(tab[:, 0:6, :], tables[0:6].rearrange("n p s -> p n s")).then_inc(mask_in, 16)
            pool.dma_start(wr[:], moe_w_router[0].rearrange("(k p) e -> p k e", p=P)).then_inc(wr_in, 16)
            for n in range(4):
                if n:
                    pool.wait_ge(tok_ok, 2 * n)
                for v, vec in enumerate((ln_g, ln_b)):
                    pool.dma_start(gb[:, v, :], vec[n // 2, n % 2:n % 2 + 1, :].to_broadcast([P, D])).then_inc(gb_in, 16)
                if n == 3:
                    break
                pool.wait_ge(gb_in, 32 * (n + 1))
                pool.wait_ge(xT_ps, HALF * TT * (n + 2))
                for v, op in enumerate((ALU.mult, ALU.add)):
                    if v:
                        pool.wait_ge(tok_ok, 2 * n + 1)
                    pool.tensor_tensor(tok[:], tok[:], gb[:, v:v + 1, :].to_broadcast([P, TT, D]), op).then_inc(tok_ok, 1)

        @block.tensor
        def _(pe):
            def piece(phase, k, rnd=0):
                pe.wait_ge(low_ok, phase.done(k + 1, rnd))
                s = phase.split(k)
                return wh[:, s, :], wl[:, s, :]

            def keep_warm(n):
                for _ in range(n):
                    pe.matmul(ps[:, 1, :], zero[:, 0:P], zero[:], start=True, stop=True)

            def product(out, stationary, moving, start, stop):
                sh, sl = stationary
                mh, ml = moving
                pe.matmul(out, sh, mh, start=start, stop=False)
                pe.matmul(out, sh, ml, start=False, stop=False)
                return pe.matmul(out, sl, mh, start=False, stop=stop)

            def turn_stream(t, h):
                for k in range(h * KD // HALF, (h + 1) * KD // HALF):
                    last = pe.transpose(banks(2 + 2 * t, 2)[:, k * P:(k + 1) * P], tok[:, t, k * P:(k + 1) * P], ident)
                last.then_inc(xT_ps, 1)

            def chan_cols(bank, phase, places, rnd=0):
                for q, n in enumerate(places):
                    hi, lo = (as_cols(w) for w in piece(phase, n, rnd))
                    for i in range(QI // P):
                        o = banks(bank, 2)[:, (2 * q + i) * SEQ:(2 * q + i + 1) * SEQ]
                        c = slice(i * P, (i + 1) * P)
                        for k in range(KD):
                            last = product(o, (hi[:, k, c], lo[:, k, c]), (chh[:, k, :], chl[:, k, :]),
                                           k == 0, k == KD - 1)
                    last.then_inc(pieces, 1)

            def rows_part(w, stationary, i, t, h, start, stop):
                c, d = slice(t * P, (t + 1) * P), slice(h * BANK, (h + 1) * BANK)
                return product(ps[:, 4 + 2 * t + h, :], [a[:, c] for a in stationary], [a[:, i, d] for a in w], start, stop)

            def tok_rows(phase, places, stationary, start, rnd=0, first=0):
                for q, n in enumerate(places):
                    w = [as_rows(a) for a in piece(phase, n, rnd)]
                    for i in range(2):
                        for t in range(TT):
                            for h in range(HALF):
                                last = rows_part(w, [a[:, first + 2 * q + i, :] for a in stationary], i, t, h,
                                                 start and q == 0 and i == 0, False)
                    last.then_inc(pieces, 1)

            def last_rows(n, phase, places, stationary, start, first=0):
                ws = []
                for t in range(TT):
                    for h in range(HALF):
                        for q, m in enumerate(places):
                            if len(ws) <= q:
                                ws.append([as_rows(a) for a in piece(phase, m)])
                            if (t, h, q) == (TT - 1, HALF - 1, 1):
                                turn_normalised(n, 0)
                            for i in range(2):
                                last = rows_part(ws[q], [a[:, first + 2 * q + i, :] for a in stationary], i, t, h,
                                                 start and q == 0 and i == 0, q == 1 and i == 1)
                            if (t, h) == (TT - 1, HALF - 1):
                                last.then_inc(pieces, 1)
                        if (t, h) != (TT - 1, HALF - 1):
                            last.then_inc(mix_part, 1)

            def turn_normalised(n, t):
                for h in range(HALF):
                    pe.wait_ge(norm_ok, HALF * (TT * n + t) + h + 1)
                    turn_stream(t, h)

            pe.wait_ge(const_set, 1)
            keep_warm(WARM_X)
            pe.wait_ge(tab_in, 16)
            for t in range(TT):
                pe.wait_ge(x_in[t], 16)
                for h in range(HALF):
                    turn_stream(t, h)
            keep_warm(WARM_W)
            pe.wait_ge(par_in, 48)
            pe.transpose(ps[:, 0, 0:NPAR], prow[0:NPAR, :], ident[0:NPAR, 0:NPAR]).then_inc(par_t, 1)

            pe.wait_ge(par_done, 1)
            pe.wait_ge(ch_low, 2 * TT)
            with pe.Fori(0, NCA) as i:
                for part, bank in enumerate((0, 6, 2)):
                    if part == 1:
                        pe.wait_ge(mixT_ok, i + 1)
                    chan_cols(bank, conv_w, (2 * part, 2 * part + 1), i)
                pe.wait_ge(gate_sb, i * 2 + 1)
            pe.wait_ge(gate_sb, NCA * 2)
            for i in range(NCA):
                pe.wait_ge(mixT_ok, i + 2)
                if i < NCA - 1:
                    tok_rows(conv_o, (2 * i, 2 * i + 1), (mixh, mixl), i == 0, first=i * CT)
                else:
                    last_rows(0, conv_o, (2 * i, 2 * i + 1), (mixh, mixl), i == 0, first=i * CT)

            def after_norm(n):
                keep_warm(WARM_NORM)
                turn_normalised(n, 1)
                keep_warm(WARM_CHAN)
                pe.wait_ge(ch_low, 2 * TT * (n + 2))

            after_norm(0)

            pe.wait_ge(const_set, 2)
            for b in range(4):
                pe.matmul(ps[:, 4 + b, :], zero[:, 0:P], zero[:], start=True, stop=False)
            chan_cols(0, dense_0, (0, 1))
            hidT = (hidh, hidl)
            with pe.Fori(0, NFULL - 1) as i:
                chan_cols(2, dense_w, (0, 1), i)
                pe.wait_ge(silu_ok, i + 1)
                chan_cols(0, dense_w, (2, 3), i)
                pe.wait_ge(hid_ok, i + 1)
                tok_rows(dense_w, (4, 5), hidT, False, i)
            chan_cols(2, dense_z, (0, 1))
            pe.wait_ge(silu_ok, NFULL)
            chan_cols(0, dense_z, (2,))
            pe.wait_ge(hid_ok, NFULL)
            chan_cols(2, dense_z, (3,))
            tok_rows(dense_z, (4,), hidT, False)
            pe.wait_ge(hid_ok, NFULL + 1)
            last_rows(1, dense_z, (5, 6), hidT, False, first=2)
            after_norm(1)

            def keys_queries(g):
                chan_cols(0, qkv_w, (0, 1), g)
                chan_cols(2, qkv_w, (2, 3), g)
                pe.wait_ge(v_ok, g + 1)

            def values(q, g):
                hi, lo = (as_cols(w) for w in piece(qkv_w, 4 + q, g))
                for t in range(TT):
                    c = slice(t * P, (t + 1) * P)
                    for k in range(KD):
                        last = product(ps[:, 4 + t, q * QI:(q + 1) * QI], (chh[:, k, c], chl[:, k, c]),
                                       (hi[:, k, :], lo[:, k, :]), k == 0, k == KD - 1)
                last.then_inc(pieces, 1)

            with pe.Fori(0, NG - 1) as g:
                keys_queries(g)
                values(0, g)
                values(1, g)
                pe.wait_ge(kq_ok, g * 2 + 2)
            keys_queries(NG - 1)
            values(0, NG - 1)
            units = [(pair, t, h) for pair in range(H // 2) for t in range(TT) for h in range(2)]

            def scores(n):
                pair, t, h = units[n]
                r = slice(HD * h, HD * h + HD)
                if n >= 2:
                    pe.wait_ge(max_ok, n - 1)
                w = (t + 1) * P
                o = banks(2 * (n % 2), 2).rearrange("p (g k) -> p g k", k=SEQ)
                for g in range(NG):
                    c = g * (AW // P) + pair
                    last = pe.matmul(o[:, g, 0:w], qryT[r, c, t * P:(t + 1) * P], keyT[r, c, 0:w], start=True, stop=True)
                last.then_inc(sc_ps, 1)

            def turn_probs(n):
                pair, t, h = units[n]
                pe.wait_ge(prob_ok, n + 1)
                if n >= 1:
                    pe.wait_ge(pT_ok, n)
                w = t + 1
                for g in range(NG):
                    for k in range(w):
                        m = g * w + k
                        last = pe.transpose(banks(4, 2)[:, m * P:(m + 1) * P], masked[n % 4][:, m * P:(m + 1) * P], ident)
                last.then_inc(pT_ps, 1)

            def outputs(n):
                pair, t, h = units[n]
                pe.wait_ge(pT_ok, n + 1)
                m = n // 2
                if h == 0 and m >= 2:
                    pe.wait_ge(o_ok, m - 1)
                w = t + 1
                for g in range(NG):
                    for k in range(w):
                        j = g * w + k
                        c = g * AW + (2 * pair + h) * HD
                        last = pe.matmul(ps[HD * h:HD * h + HD, 6 + m % 2, 0:P], val[:, k, c:c + HD],
                                         probT[:, n % 2, j * P:(j + 1) * P], start=(j == 0), stop=(j == NG * w - 1))
                last.then_inc(o_ps, 1)

            pe.wait_ge(kq_ok, NG * 2)
            scores(0)
            scores(1)
            values(1, NG - 1)
            pe.wait_ge(v_ok, NG + 1)
            N = len(units)
            for n in range(N + 3):
                if 2 <= n < N:
                    scores(n)
                if 2 <= n < N + 2:
                    turn_probs(n - 2)
                if n >= 3:
                    outputs(n - 3)
            pe.wait_ge(o_ok, H // 2 * TT)
            pe.wait_ge(max_ok, N)
            last_rows(2, att_o, (0, 1), (atth, attl), True)
            keep_warm(WARM_NORM)
            turn_normalised(2, 1)

            pe.wait_ge(wr_in, 16)
            for t in range(TT):
                pe.wait_ge(chan_d, TT * 3 + t + 1)
                pe.wait_ge(chan_a, TT * 3 + t + 1)
                for k in range(KD):
                    last = pe.matmul(ps[:, 0, t * E:(t + 1) * E], chan[:, k, t * P:(t + 1) * P], wr[:, k, :],
                                     start=(k == 0), stop=(k == KD - 1))
            last.then_inc(log_ps, 1)
            keep_warm(WARM_ROUTER)
            pe.wait_ge(sel_ok, 1)
            pe.matmul(ps[:, 1, 0:E], tri, sel[:, :, 0], start=True, stop=True)
            pe.matmul(ps[:, 1, E:2 * E], tri, sel[:, :, 1], start=True, stop=False)
            pe.matmul(ps[:, 1, E:2 * E], ones[:], sel[:, :, 0], start=False, stop=True)
            pe.matmul(ps[:, 1, 2 * E:3 * E], ones[:], sel[:, :, 0], start=True, stop=False)
            pe.matmul(ps[:, 1, 2 * E:3 * E], ones[:], sel[:, :, 1], start=False, stop=True).then_inc(rank_ps, 1)
            pe.wait_ge(tok_ok, 2 * 3)

            def gather():
                for k in range(KD):
                    for t in range(TT):
                        last = pe.matmul(banks(2, 2)[:, k * P:(k + 1) * P], tok[:, t, k * P:(k + 1) * P],
                                         pick[:, t, :], start=(t == 0), stop=(t == TT - 1))
                last.then_inc(xe_ps, 1)

            def expert(j, final=False):
                def gate_up(c, part):
                    for q in range(2):
                        hi, lo = (as_cols(w) for w in piece(expert_w, AT[("gate", "up")[part], c] + q, j))
                        for k in range(KD):
                            last = product(ps[:, 2 * (c % 2) + part, q * QI:(q + 1) * QI], (xeh[:, k, :], xel[:, k, :]),
                                           (hi[:, k, :], lo[:, k, :]), k == 0, k == KD - 1)
                        last.then_inc(pieces, 1)

                def turn_hid(c):
                    pe.wait_ge(ehid, j * NC + c + 1)
                    for i in range(CT):
                        last = pe.transpose(ps[:, 6, i * P:(i + 1) * P], hid[:, i * P:(i + 1) * P], ident)
                    last.then_inc(ht_ps, 1)

                def down(c):
                    pe.wait_ge(ht_ok, j * NC + c + 1)
                    for q in range(2):
                        hi, lo = (as_rows(w) for w in piece(expert_w, AT["down", c] + q, j))
                        for i in range(2):
                            n = 2 * q + i
                            b = slice(n * P, (n + 1) * P)
                            for h in range(HALF):
                                d = slice(h * BANK, (h + 1) * BANK)
                                last = product(ps[:, 4 + h, :], (hTh[:, c % 2, b], hTl[:, c % 2, b]),
                                               (hi[:, i, d], lo[:, i, d]), c == 0 and n == 0, c == NC - 1 and n == CT - 1)
                        last.then_inc(pieces, 1)

                pe.wait_ge(xe_ok, j + 1)
                for c in range(NC):
                    if c == 1:
                        pe.wait_ge(comb_ok, j * 2 + 1)
                    gate_up(c, 0)
                    if c:
                        turn_hid(c - 1)
                    gate_up(c, 1)
                    if c:
                        down(c - 1)
                    if c == 2:
                        pe.wait_ge(wsel_ok, j + 1)
                        for t in range(TT):
                            last = pe.transpose(ps[:, 7, t * P:(t + 1) * P], wsel[:, t, :], ident)
                        last.then_inc(wT_ps, 1)
                turn_hid(NC - 1)
                if not final:
                    pe.wait_ge(pick_ok, j + 2)
                    gather()
                down(NC - 1)
                pe.wait_ge(ye_ok, j * 2 + 2)
                pe.wait_ge(wT_ok, j + 1)
                if not final:
                    pe.wait_ge(xe_ok, j + 2)
                for t in range(TT):
                    for h in range(HALF):
                        last = pe.matmul(ps[:, 2 * t + h, :], back[:, t * P:(t + 1) * P], ye[:, h * BANK:(h + 1) * BANK],
                                         start=True, stop=True)
                    last.then_inc(comb_ps, 1)
                pe.wait_ge(comb_ok, j * 2 + 2)

            pe.wait_ge(pick_ok, 1)
            gather()
            pe.wait_ge(flag_ok, 1)
            keep_warm(WARM_XE)
            with pe.Fori(0, E - 1) as j:
                expert(j)
            expert(E - 1, final=True)
            over = pe.value_load(flag[0:1, 0:1], min_val=0, max_val=1)
            with pe.If(over > 0):
                pe.wait_ge(pick_ok, E + 1)
                pe.wait_ge(comb_ok, 2 * E + 1)
                gather()
                with pe.Fori(E, 2 * E - 1) as j:
                    expert(j)
                expert(2 * E - 1, final=True)
            with pe.Else():
                pe.nop()

        @block.scalar
        def _(act):
            G, B = 0, 4 * KD

            def round_piece(phase, k, rnd=0):
                act.wait_ge(landed[phase.slot(k)], phase.landed(k, rnd))
                if not isinstance(rnd, int) or phase.done(k, rnd) >= SPLIT:
                    act.wait_ge(pieces, phase.done(k + 1 - SPLIT, rnd))
                act.copy(wh[:, phase.split(k), :], phase.raw(k)).then_inc(high_ok, 1)

            def chan_tile(n, t):
                c = slice(t * P, (t + 1) * P)
                src = ps[:, 3 + 2 * t, :].rearrange("p (k t) -> p k t", t=P)
                act.wait_ge(xT_ps, HALF * (TT * n + t) + 2)
                if n == 0:
                    act.copy(chan[:, 4:8, c], src).then_inc(chan_a, 1)
                else:
                    for k in range(4, 8):
                        m = (n - 1) * KD + k
                        last = act.activation(chan[:, k, c], src[:, k - 4, :], ACT.Identity, scale=pcol[:, G + m:G + m + 1],
                                              bias=pcol[:, B + m:B + m + 1])
                    last.then_inc(chan_a, 1)
                if n < 3:
                    act.wait_ge(chan_a, TT * n + t + 1)
                    act.copy(chh[:, 4:8, c], chan[:, 4:8, c]).then_inc(ch_high, 1)

            def round_dve_half(n, t):
                c = slice(t * P, (t + 1) * P)
                act.wait_ge(chan_d, TT * n + t + 1)
                act.copy(chh[:, 0:4, c], chan[:, 0:4, c]).then_inc(ch_high, 1)

            def scale_rows(n, t):
                act.wait_ge(var_ok, TT * n + t + 1)
                act.activation(mv[:, t, 2:3], mv[:, t, 1:2], ACT.Sqrt).then_inc(dev_ok, 1)
                act.wait_ge(res_ok, TT * n + t + 1)
                for h in range(HALF):
                    d = slice(h * BANK, (h + 1) * BANK)
                    act.activation(tok[:, t, d], res[:, t, d], ACT.Identity, scale=mv[:, t, 2:3],
                                   bias=mv[:, t, 3:4]).then_inc(norm_ok, 1)

            def normalise(n, phase, k):
                scale_rows(n, 0)
                chan_tile(n + 1, 0)
                scale_rows(n, 1)
                if n < 2:
                    round_dve_half(n + 1, 0)
                chan_tile(n + 1, 1)
                if n < 2:
                    round_dve_half(n + 1, 1)
                round_piece(phase, k)

            for t in range(TT):
                chan_tile(0, t)
                round_dve_half(0, t)
            for k in range(3):
                round_piece(conv_w, k)
            with act.Fori(0, NCA) as i:
                round_piece(conv_w, 3, i)
                round_piece(conv_w, 4, i)
                act.wait_ge(pieces, conv_w.done(2, i))
                act.wait_ge(mixT_ok, i + 1)
                act.copy(gateB, banks(0, 2).rearrange("p (c t) -> p c t", c=CT)).then_inc(gate_sb, 1)
                round_piece(conv_w, 5, i)
                round_piece(conv_w, 6, i)
                act.wait_ge(pieces, conv_w.done(4, i))
                act.copy(gateC, banks(6, 2).rearrange("p (c t) -> p c t", c=CT)).then_inc(gate_sb, 1)
                round_piece(conv_w, 7, i)
                round_piece(conv_w, 8, i)
            round_piece(conv_o, 3)
            round_piece(dense_0, 0)
            normalise(0, dense_0, 1)

            def silu_dense(i, width, done):
                act.wait_ge(pieces, done)
                if not isinstance(i, int) or i > 0:
                    act.wait_ge(hid_ok, i)
                act.activation(sgd[:, 0:width], banks(0, 2)[:, 0:width], ACT.Silu).then_inc(silu_ok, 1)

            round_piece(dense_w, 0)
            round_piece(dense_w, 1)
            silu_dense(0, CT * SEQ, dense_0.done(2))
            with act.Fori(0, NFULL - 1) as i:
                for k in (2, 3, 4, 5):
                    round_piece(dense_w, k, i)
                silu_dense(i + 1, CT * SEQ, dense_w.done(4, i))
                for k in (6, 7):
                    round_piece(dense_w, k, i)
            for k in (2, 3, 4):
                round_piece(dense_z, k)
            silu_dense(NFULL, QI // P * SEQ, dense_z.done(3))
            for k in (5, 6, 7):
                round_piece(dense_z, k)
            normalise(1, dense_z, 8)

            with act.Fori(0, NG) as g:
                round_piece(qkv_w, 2, g)
                round_piece(qkv_w, 3, g)
                act.wait_ge(pieces, qkv_w.done(2, g))
                act.copy(keyT[:, bass.ds(g * CT, CT), :], banks(0, 2).rearrange("p (c t) -> p c t", c=CT)).then_inc(kq_ok, 1)
                round_piece(qkv_w, 4, g)
                round_piece(qkv_w, 5, g)
                act.wait_ge(pieces, qkv_w.done(4, g))
                act.copy(qryT[:, bass.ds(g * CT, CT), :], banks(2, 2).rearrange("p (c t) -> p c t", c=CT)).then_inc(kq_ok, 1)
                round_piece(qkv_w, 6, g)
                round_piece(qkv_w, 7, g)

            def exp_unit(n):
                w = NG * ((n // 2 % 2) + 1) * P
                act.wait_ge(max_ok, n + 1)
                act.activation(masked[n % 4][:, 0:w], masked[n % 4][:, 0:w], ACT.Exp, scale=SCALE,
                               bias=soft[:, n % 2, 1:2], accum_out=soft[:, n % 2, 2:3]).then_inc(exp_ok, 1)

            def copy_probs(n):
                w = NG * ((n // 2 % 2) + 1) * P
                act.wait_ge(pT_ps, n + 1)
                if n >= 2:
                    act.wait_ge(o_ps, n - 1)
                act.copy(probT[:, n % 2, 0:w], banks(4, 2)[:, 0:w]).then_inc(pT_ok, 1)

            for n in range(TT * H + 2):
                if n < TT * H:
                    exp_unit(n)
                if n >= 2:
                    copy_probs(n - 2)
            round_piece(expert_w, 0)
            normalise(2, expert_w, 1)
            round_piece(expert_w, 2)

            act.wait_ge(lgap_ok, 1)
            act.activation(gate2[:, 1, :], gate2[:, 0, :], ACT.Exp).then_inc(lexp_ok, 1)

            def round_xe(n):
                act.wait_ge(xe_ps, n)
                act.copy(xeh, banks(2, 2).rearrange("p (k s) -> p k s", k=KD)).then_inc(xe_high, 1)

            def expert(j, final=False):
                for n in range(3, PER_EXPERT):
                    part, c = ORDER[n // 2]
                    if n == AT["gate", 1]:
                        silu(j, 0)
                    if part == "down" and c < NC - 1 and n % 2 == 0:
                        silu(j, c + 1)
                        round_hid(j, c)
                    if n == AT["down", 2]:
                        act.wait_ge(wT_ps, j + 1)
                        act.copy(back, ps[:, 7, 0:SEQ]).then_inc(wT_ok, 1)
                    round_piece(expert_w, n, j)
                round_hid(j, NC - 1)
                if not final:
                    round_xe(j + 2)
                    for n in range(2):
                        round_piece(expert_w, PER_EXPERT + n, j)
                act.wait_ge(pieces, expert_w.done(PER_EXPERT, j))
                act.copy(ye[:, 0:BANK], ps[:, 4, :]).then_inc(ye_ok, 1)
                if not final:
                    round_piece(expert_w, PER_EXPERT + 2, j)

            def silu(j, c):
                act.wait_ge(pieces, expert_w.done(AT["gate", c] + 2, j))
                act.activation(sg[:, c % 2, :], ps[:, 2 * (c % 2), :], ACT.Silu).then_inc(esilu, 1)

            def round_hid(j, c):
                act.wait_ge(ht_ps, j * NC + c + 1)
                act.copy(hTh[:, c % 2, :], ps[:, 6, :]).then_inc(ht_high, 1)

            round_xe(1)
            with act.Fori(0, E - 1) as j:
                expert(j)
            expert(E - 1, final=True)
            act.wait_ge(flag_ok, 1)
            over = act.value_load(flag[0:1, 0:1], min_val=0, max_val=1)
            with act.If(over > 0):
                for n in range(3):
                    round_piece(expert_w, n, E)
                round_xe(E + 1)
                with act.Fori(E, 2 * E - 1) as j:
                    expert(j)
                expert(2 * E - 1, final=True)
            with act.Else():
                act.nop()
            for t in range(TT):
                act.wait_ge(var_ok, TT * 3 + t + 1)
                act.activation(mv[:, t, 2:3], mv[:, t, 1:2], ACT.Sqrt).then_inc(dev_ok, 1)

        @block.vector
        def _(dve):
            chain = Chain(dve, dve_steps)
            G, B, C = 0, 4 * KD, 8 * KD

            def rest_piece(phase, k, rnd=0):
                dve.wait_ge(high_ok, phase.done(k + 1, rnd))
                s = phase.split(k)
                dve.tensor_tensor(wl[:, s, :], phase.raw(k), wh[:, s, :].bitcast(F32),
                                  ALU.subtract).then_inc(low_ok, 1)

            def chan_tile(n, t):
                c = slice(t * P, (t + 1) * P)
                src = ps[:, 2 + 2 * t, :].rearrange("p (k t) -> p k t", t=P)
                dve.wait_ge(xT_ps, HALF * (TT * n + t) + 1)
                if n == 0:
                    dve.tensor_copy(chan[:, 0:4, c], src).then_inc(chan_d, 1)
                else:
                    for k in range(4):
                        m = (n - 1) * KD + k
                        last = dve.tensor_scalar(chan[:, k, c], src[:, k, :], pcol[:, G + m:G + m + 1],
                                                 pcol[:, B + m:B + m + 1], ALU.mult, ALU.add)
                    last.then_inc(chan_d, 1)
                for m, half in enumerate((slice(4, 8), slice(0, 4)) if n < 3 else ()):
                    dve.wait_ge(ch_high, TT * 2 * n + 2 * t + m + 1)
                    if m:
                        dve.wait_ge(chan_d, TT * n + t + 1)
                    dve.tensor_tensor(chl[:, half, c], chan[:, half, c], chh[:, half, c].bitcast(F32),
                                      ALU.subtract).then_inc(ch_low, 1)

            def half_rows(t, h):
                return dve.bn_stats(stats[:, t, h, :], res[:, t, h * BANK:(h + 1) * BANK])

            def variance(t, last):
                chain.link(last)
                chain.link(dve.bn_aggr(mv[:, t, 0:2], stats[:, t, :, :]))
                dve.tensor_scalar(mv[:, t, 1:2], mv[:, t, 1:2], EPS, None, ALU.add).then_inc(var_ok, 1)

            def scales(n, t):
                dve.wait_ge(dev_ok, TT * n + t + 1)
                chain.link(dve.reciprocal(mv[:, t, 2:3], mv[:, t, 2:3]))
                dve.tensor_scalar(mv[:, t, 3:4], mv[:, t, 0:1], mv[:, t, 2:3], -1.0, ALU.mult, ALU.mult).then_inc(res_ok, 1)

            def residual(n, done):
                if n:
                    dve.wait_ge(tok_ok, 2 * n)
                for t in range(TT):
                    for h in range(HALF):
                        if (t, h) == (TT - 1, HALF - 1):
                            dve.wait_ge(pieces, done)
                        else:
                            dve.wait_ge(mix_part, (HALF * TT - 1) * n + HALF * t + h + 1)
                        d = slice(h * BANK, (h + 1) * BANK)
                        chain.link(dve.scalar_tensor_tensor(out=res[:, t, d], in0=tok[:, t, d], scalar=ALPHA,
                                                            in1=ps[:, 4 + 2 * t + h, :], op0=ALU.mult, op1=ALU.add))
                        last = half_rows(t, h)
                    variance(t, last)
                    scales(n, t)
                for t in range(TT):
                    chan_tile(n + 1, t)

            dve.memset(upad[:, :, 0:CW - 1], 0.0).then_inc(mixT_ok, 1)
            for t in range(TT):
                chan_tile(0, t)
            dve.wait_ge(par_t, 1)
            dve.tensor_copy(pcol[:], ps[:, 0, 0:NPAR]).then_inc(par_done, 1)
            dve.memset(soft[:], 0.0).then_inc(v_ok, 1)
            for k in range(3):
                rest_piece(conv_w, k)

            def taps(w, i, c):
                return pcol[:, bass.ds(i * CT + (C + w * KD + c), 1)]

            with dve.Fori(0, NCA) as i:
                for k in range(3, 8):
                    rest_piece(conv_w, k, i)
                dve.wait_ge(pieces, conv_w.done(6, i))
                dve.wait_ge(gate_sb, i * 2 + 2)
                dve.tensor_tensor(upad[:, :, CW - 1:], banks(2, 2).rearrange("p (c t) -> p c t", c=CT), gateC,
                                  ALU.mult).then_inc(u_read, 1)
                dve.wait_ge(u_read, i + 1)
                for c in range(CT):
                    last = dve.tensor_scalar(conv[:, c, :], upad[:, c, 0:SEQ], taps(0, i, c), None, ALU.mult)
                last.then_inc(conv_ok, 1)
                rest_piece(conv_w, 8, i)
                for w in range(1, CW):
                    dve.wait_ge(conv_ok, i * CW + w)
                    for c in range(CT):
                        last = dve.scalar_tensor_tensor(out=conv[:, c, :], in0=upad[:, c, w:w + SEQ], scalar=taps(w, i, c),
                                                        in1=conv[:, c, :], op0=ALU.mult, op1=ALU.add)
                    last.then_inc(conv_ok, 1)
                dve.wait_ge(conv_ok, i * CW + CW)
                dve.tensor_tensor(conv, conv, gateB, ALU.mult).then_inc(msplit, 1)
                dve.wait_ge(msplit, i * 2 + 1)
                dve.tensor_copy(mixh[:, bass.ds(i * CT, CT), :], conv).then_inc(msplit, 1)
                dve.wait_ge(msplit, i * 2 + 2)
                dve.tensor_tensor(mixl[:, bass.ds(i * CT, CT), :], conv, mixh[:, bass.ds(i * CT, CT), :].bitcast(F32),
                                  ALU.subtract).then_inc(mixT_ok, 1)
            rest_piece(conv_o, 3)
            rest_piece(dense_0, 0)
            residual(0, conv_o.done(4))
            rest_piece(dense_0, 1)

            def hidden(i, w, done, at=0):
                dve.wait_ge(silu_ok, i + 1)
                dve.wait_ge(pieces, done)
                flat = [a.rearrange("p c t -> p (c t)")[:, at:at + w] for a in (hidh, hidl)]
                dve.tensor_tensor(sgd[:, 0:w], banks(2, 2)[:, 0:w], sgd[:, 0:w], ALU.mult).then_inc(hsplit, 1)
                dve.wait_ge(hsplit, i * 2 + 1)
                dve.tensor_copy(flat[0], sgd[:, 0:w]).then_inc(hsplit, 1)
                dve.wait_ge(hsplit, i * 2 + 2)
                dve.tensor_tensor(flat[1], sgd[:, 0:w], flat[0].bitcast(F32), ALU.subtract).then_inc(hid_ok, 1)

            rest_piece(dense_w, 0)
            rest_piece(dense_w, 1)
            with dve.Fori(0, NFULL - 1) as i:
                rest_piece(dense_w, 2, i)
                rest_piece(dense_w, 3, i)
                hidden(i, CT * SEQ, dense_w.done(2, i))
                for k in range(4, 8):
                    rest_piece(dense_w, k, i)
            rest_piece(dense_z, 2)
            rest_piece(dense_z, 3)
            hidden(NFULL - 1, CT * SEQ, dense_z.done(2))
            rest_piece(dense_z, 4)
            rest_piece(dense_z, 5)
            hidden(NFULL, QI // P * SEQ, dense_z.done(4), at=CT * SEQ)
            rest_piece(dense_z, 6)
            rest_piece(dense_z, 7)
            residual(1, dense_z.done(7))
            rest_piece(dense_z, 8)

            def keep_values(g):
                dve.wait_ge(pieces, qkv_w.done(6, g))
                dve.tensor_copy(val[:, :, bass.ds(g * AW, AW)], ps[:, 4:4 + TT, :]).then_inc(v_ok, 1)

            with dve.Fori(0, NG - 1) as g:
                for k in range(2, 8):
                    rest_piece(qkv_w, k, g)
                keep_values(g)
            for k in range(2, 8):
                rest_piece(qkv_w, k, NG - 1)

            def maximum(n):
                t = n // 2 % 2
                w = (t + 1) * P
                dve.wait_ge(sc_ps, n + 1)
                if n >= 4:
                    dve.wait_ge(pT_ps, n - 3)
                src = banks(2 * (n % 2), 2)[:, 0:NG * SEQ].rearrange("p (g k) -> p g k", g=NG)[:, :, 0:w]
                m = (masks if t else masks[:, :, 1:2, :]).rearrange("p g k s -> p g (k s)") if t else masks[:, :, 1, :]
                dst = masked[n % 4][:, 0:NG * w].rearrange("p (g k) -> p g k", g=NG)
                chain.link(dve.tensor_tensor_reduce(out=dst, in0=src, in1=m, scale=1.0, scalar=-3.0e38,
                                                    op0=ALU.add, op1=ALU.max, accum_out=soft[:, n % 2, 0:1]))
                dve.tensor_scalar(soft[:, n % 2, 1:2], soft[:, n % 2, 0:1], -SCALE, None, ALU.mult).then_inc(max_ok, 1)

            def divide(n):
                w = NG * ((n // 2 % 2) + 1) * P
                dve.wait_ge(exp_ok, n + 1)
                chain.link(dve.reciprocal(soft[:, n % 2, 3:4], soft[:, n % 2, 2:3]))
                dve.tensor_scalar(masked[n % 4][:, 0:w], masked[n % 4][:, 0:w], soft[:, n % 2, 3:4], None,
                                  ALU.mult).then_inc(prob_ok, 1)

            def keep_outputs(m):
                dve.wait_ge(o_ps, 2 * m + 2)
                t = m % TT
                c = slice(t * P, (t + 1) * P)
                src = ps[:, 6 + m % 2, 0:P]
                chain.link(dve.tensor_copy(atth[:, m // TT, c], src))
                dve.tensor_tensor(attl[:, m // TT, c], src, atth[:, m // TT, c].bitcast(F32), ALU.subtract).then_inc(o_ok, 1)

            N = H * TT
            dve.wait_ge(mask_in, 16)
            maximum(0)
            maximum(1)
            keep_values(NG - 1)
            for n in range(N + 4):
                if 2 <= n < N:
                    maximum(n)
                if 1 <= n <= N:
                    divide(n - 1)
                if n >= 4 and (n - 4) % 2 == 1:
                    keep_outputs((n - 4) // 2)
            rest_piece(expert_w, 0)
            residual(2, att_o.done(2))

            dve.wait_ge(log_ps, 1)
            dve.tensor_copy(lg[:], ps[:, 0, 0:TT * E].rearrange("p (t e) -> p t e", t=TT))
            chain.link(dve.tensor_scalar(prio[:], slots[:, 0:E], -1.0, float(P), ALU.mult, ALU.add))
            for choice in range(2):
                chain.link(dve.tensor_reduce(top[:, choice, :], lg[:], AX_X, ALU.max))
                for t in range(TT):
                    last = dve.scalar_tensor_tensor(out=pr[:, t, :], in0=lg[:, t, :], scalar=top[:, choice, t:t + 1],
                                                    in1=prio[:], op0=ALU.is_equal, op1=ALU.mult)
                chain.link(last)
                chain.link(dve.tensor_reduce(pm[:], pr[:], AX_X, ALU.max))
                for t in range(TT):
                    last = dve.tensor_scalar(hot[:, choice, t, :], pr[:, t, :], pm[:, t:t + 1], None, ALU.is_equal)
                chain.link(last)
                if choice == 0:
                    chain.link(dve.scalar_tensor_tensor(out=lg[:], in0=hot[:, 0, :, :], scalar=-3.0e38, in1=lg[:],
                                                        op0=ALU.mult, op1=ALU.add))
            dve.tensor_tensor(gate2[:, 0, :], top[:, 1, :], top[:, 0, :], ALU.subtract).then_inc(lgap_ok, 1)
            dve.tensor_tensor(sel[:, :, :], hot[:, 0, :, :].rearrange("p t e -> p e t"),
                              hot[:, 1, :, :].rearrange("p t e -> p e t"), ALU.add).then_inc(sel_ok, 1)
            dve.wait_ge(lexp_ok, 1)
            chain.link(dve.tensor_scalar(gate2[:, 3, :], gate2[:, 1, :], 1.0, None, ALU.add))
            chain.link(dve.reciprocal(gate2[:, 2, :], gate2[:, 3, :]))
            chain.link(dve.tensor_tensor(gate2[:, 3, :], gate2[:, 1, :], gate2[:, 2, :], ALU.mult))
            for t in range(TT):
                last = dve.tensor_scalar(comb[:, :, t], hot[:, 0, t, :], gate2[:, 2, t:t + 1], None, ALU.mult)
            chain.link(last)
            for t in range(TT):
                dve.scalar_tensor_tensor(out=comb[:, :, t], in0=hot[:, 1, t, :], scalar=gate2[:, 3, t:t + 1],
                                         in1=comb[:, :, t], op0=ALU.mult, op1=ALU.add)
            dve.wait_ge(rank_ps, 1)
            chain.link(dve.tensor_copy(rank[:], ps[:, 1, 0:TT * E].rearrange("p (t e) -> p e t", t=TT)))

            def picker(dst, e, values, done):
                for t in range(TT):
                    last = dve.tensor_scalar(dst[:, t, :], slots, rank[:, bass.ds(e, 1), t], values[:, bass.ds(e, 1), t],
                                             ALU.is_equal, ALU.mult)
                last.then_inc(done, 1)

            picker(pick, 0, sel, pick_ok)
            chain.link(dve.tensor_reduce(peak[:], ps[:, 1, 2 * E:3 * E], AX_X, ALU.max))
            chain.link(dve.tensor_scalar(flag[:], peak[:], float(P), None, ALU.is_gt))
            dve.wait_ge(tok_ok, 2 * 3)
            dve.tensor_scalar(res[:], tok[:], ALPHA, None, ALU.mult).then_inc(comb_ok, 1)
            dve.engine_nop().then_inc(flag_ok, 1)
            rest_piece(expert_w, 1)

            def rest_xe(n):
                dve.wait_ge(xe_high, n)
                dve.tensor_tensor(xel, banks(2, 2).rearrange("p (k s) -> p k s", k=KD), xeh.bitcast(F32),
                                  ALU.subtract).then_inc(xe_ok, 1)

            def expert(j, e, final=False):
                def rest_hid(c):
                    dve.wait_ge(ht_high, j * NC + c + 1)
                    dve.tensor_tensor(hTl[:, c % 2, :], ps[:, 6, :], hTh[:, c % 2, :].bitcast(F32),
                                      ALU.subtract).then_inc(ht_ok, 1)

                def hidden(c):
                    dve.wait_ge(esilu, j * NC + c + 1)
                    dve.wait_ge(pieces, expert_w.done(AT["up", c] + 2, j))
                    dve.tensor_tensor(hid, ps[:, 2 * (c % 2) + 1, :], sg[:, c % 2, :], ALU.mult).then_inc(ehid, 1)

                for n in range(3, PER_EXPERT):
                    part, c = ORDER[n // 2]
                    if n == 3:
                        picker(wsel, e, comb, wsel_ok)
                        if not final:
                            picker(pick, e + 1, sel, pick_ok)
                    if n % 2 == 0 and part == "down" and c < NC - 1:
                        rest_hid(c)
                    for h in range(NC):
                        if n == AT["up", h] + 4:
                            hidden(h)
                    if final and n == PER_EXPERT - 1:
                        rest_hid(NC - 1)
                    rest_piece(expert_w, n, j)
                if not final:
                    rest_hid(NC - 1)
                    rest_xe(j + 2)
                    rest_piece(expert_w, PER_EXPERT, j)
                dve.wait_ge(pieces, expert_w.done(PER_EXPERT, j))
                dve.tensor_copy(ye[:, BANK:D], ps[:, 5, :]).then_inc(ye_ok, 1)
                if not final:
                    rest_piece(expert_w, PER_EXPERT + 1, j)
                for t in range(TT):
                    dve.wait_ge(comb_ps, j * 2 + t + 1)
                    dve.tensor_tensor(res[:, t, :], banks(2 * t, 2), res[:, t, :], ALU.add).then_inc(comb_ok, 1)
                dve.wait_ge(comb_ok, j * 2 + 3)
                if not final:
                    rest_piece(expert_w, PER_EXPERT + 2, j)

            rest_xe(1)
            rest_piece(expert_w, 2)
            with dve.Fori(0, E - 1) as j:
                expert(j, j)
            over = dve.value_load(flag[0:1, 0:1], min_val=0, max_val=1)
            expert(E - 1, E - 1, final=True)
            with dve.If(over > 0):
                dve.tensor_scalar(rank[:], rank[:], -float(P), None, ALU.add).then_inc(rank_ok, 1)
                dve.wait_ge(rank_ok, 1)
                picker(pick, 0, sel, pick_ok)
                for n in range(3):
                    rest_piece(expert_w, n, E)
                rest_xe(E + 1)
                with dve.Fori(E, 2 * E - 1) as j:
                    expert(j, j - E)
                expert(2 * E - 1, E - 1, final=True)
            with dve.Else():
                dve.nop()
            for t in range(TT):
                for h in range(HALF):
                    last = half_rows(t, h)
                variance(t, last)
                dve.wait_ge(gb_in, 32 * 4)
                chain.link(dve.scalar_tensor_tensor(out=res[:, t, :], in0=res[:, t, :], scalar=mv[:, t, 0:1],
                                                    in1=gb[:, 0, :], op0=ALU.subtract, op1=ALU.mult))
                dve.wait_ge(dev_ok, TT * 3 + t + 1)
                chain.link(dve.reciprocal(mv[:, t, 2:3], mv[:, t, 2:3]))
                for h in range(HALF):
                    d = slice(h * BANK, (h + 1) * BANK)
                    dve.scalar_tensor_tensor(out=res[:, t, d], in0=res[:, t, d], scalar=mv[:, t, 2:3], in1=gb[:, 1, d],
                                             op0=ALU.mult, op1=ALU.add).then_inc(fin_ok, 1)


def launch_tables(P, window_spans):
    import numpy as np

    q = np.arange(P)[:, None]
    k = np.arange(P)[None, :]
    out = []
    for span, dil in window_spans:
        for back in (P, 0):
            dist = back + q - k
            ok = (dist >= 0) & (dist % dil == 0) & (dist <= span * dil)
            out.append(np.where(ok, 0.0, FAR))
    out.append(np.eye(P))
    out.append(q < k)
    out.append(np.broadcast_to(k, (P, P)))
    return np.stack([np.asarray(a, np.float32) for a in out])


_INS = ['x', 'a_w_in', 'a_conv', 'a_w_out', 'kv_w', 'b_w_q', 'b_w_o', 'ffn_w_gate', 'ffn_w_up', 'ffn_w_down',
        'moe_w_router', 'moe_w_gate', 'moe_w_up', 'moe_w_down', 'ln_g', 'ln_b']


def kernel(**inputs):
    import numpy as _np
    import concourse.bacc as _bacc
    from concourse import mybir as _mybir
    from concourse.bass_utils import run_bass_kernel_spmd as _run

    nc = _bacc.Bacc("TRN2", target_bir_lowering=False, num_devices=1)
    arrays, args = {}, []
    for name in _INS:
        a = _np.ascontiguousarray(inputs[name])
        arrays[f"in_{name}_dram"] = a
        args.append(nc.dram_tensor(f"in_{name}_dram", a.shape, _mybir.dt.from_np(a.dtype), kind="ExternalInput").ap())
    tables = launch_tables(128, ((128, 1), (128, 4), (128, 16)))
    arrays["tables_dram"] = tables
    args.append(nc.dram_tensor("tables_dram", tables.shape, _mybir.dt.float32, kind="ExternalInput").ap())
    args.append(nc.dram_tensor("out_0_dram", inputs["x"].shape, _mybir.dt.float32, kind="ExternalOutput").ap())
    hybrid_trunk(nc, *args)
    r = _run(nc, [arrays], core_ids=[0])
    return r.results[0]["out_0_dram"]
```
